# Optimizing a Trainium2 kernel written in Bass

```python
import math
import jax, jax.numpy as jnp
from jax import lax
import numpy as np

D_MODEL = 2048
BATCH = 1
SEQ = 256
DEPTH = 2

CHUNK = 64
N_MIXERS = 2
N_A = (DEPTH + 1) // 2
N_B = DEPTH // 2
RMS_EPS = 1e-6

A_HEAD = 64
A_HEADS = D_MODEL // A_HEAD
A_DECAY_LORA = max(32, int(round(1.8 * D_MODEL ** 0.5 / 32)) * 32)
A_AAA_LORA = max(32, int(round(1.8 * D_MODEL ** 0.5 / 32)) * 32)
A_MV_LORA = max(32, int(round(1.3 * D_MODEL ** 0.5 / 32)) * 32)
A_GATE_LORA = max(32, int(round(0.6 * D_MODEL ** 0.8 / 32)) * 32)
A_GN_EPS = A_HEAD * 1e-5

B_HEADS = 16
B_HEAD_DIM = 128
B_KV_RANK = 512
B_IDX_HEADS = 8
B_IDX_DIM = 128
TOPK_MAX = 256
Q_BLOCK = 128
B_Q_W = B_HEADS * B_HEAD_DIM
B_QI_W = B_IDX_HEADS * B_IDX_DIM
B_IN_W = B_Q_W + B_KV_RANK + B_QI_W + B_IDX_DIM + B_IDX_HEADS
B_SCALE = B_HEAD_DIM ** -0.5
B_IDX_W_SCALE = (B_IDX_HEADS ** -0.5) * (B_IDX_DIM ** -0.5)

D_FF = ((8 * D_MODEL // 3 + 255) // 256) * 256

kernel_name = 'hybrid_rwkv7_dsa_adaln_encoder'

def _rmsnorm(x):
    xf = x.astype(jnp.float32)
    return (xf * lax.rsqrt(jnp.mean(xf * xf, axis=-1, keepdims=True) + RMS_EPS)).astype(x.dtype)

def _modulate(x, shift, scale):
    return _rmsnorm(x) * (1 + scale[:, None, :]) + shift[:, None, :]

def _rwkv7_scan(r, w, k, v, kk, a):
    B, T, H, N = r.shape

    def step(S, inp):
        r_t, w_t, k_t, v_t, kk_t, a_t = inp
        sa = jnp.einsum('bhij,bhj->bhi', S, -kk_t)
        S = (S * w_t[:, :, None, :]
             + sa[..., None] * (kk_t * a_t)[:, :, None, :]
             + v_t[..., None] * k_t[:, :, None, :])
        y = jnp.einsum('bhij,bhj->bhi', S, r_t)
        return S, y

    xs = tuple(jnp.moveaxis(t, 1, 0) for t in (r, w, k, v, kk, a))
    S0 = jnp.zeros((B, H, N, N), jnp.float32)
    _, ys = lax.scan(step, S0, xs)
    return jnp.moveaxis(ys, 0, 1)

def _rwkv7_mixer(h, v_first, mu, w_rkv, w0, w1, w2, a0, a1, a2, g1, g2,
                 k_k, k_a, r_k, ln_w, ln_b, w_o, vres):
    B, T, D = h.shape
    f32 = jnp.float32
    h_prev = jnp.pad(h, ((0, 0), (1, 0), (0, 0)))[:, :T]
    dx = h_prev - h
    xr, xw, xk, xv, xa, xg = (h + dx * mu[i] for i in range(6))
    r = xr @ w_rkv[0]
    k = xk @ w_rkv[1]
    v = xv @ w_rkv[2]
    w_log = -jax.nn.softplus(-(w0 + jnp.tanh(xw @ w1) @ w2).astype(f32)) - 0.5
    decay = jnp.exp(-jnp.exp(w_log))
    if vres is None:
        v_first = v
    else:
        v0, v1, v2 = vres
        v = v + (v_first - v) * jax.nn.sigmoid(v0 + (xv @ v1) @ v2)
    a = jax.nn.sigmoid((a0 + (xa @ a1) @ a2).astype(f32))
    g = jax.nn.sigmoid(xg @ g1) @ g2

    def heads(t):
        return t.astype(f32).reshape(B, T, A_HEADS, A_HEAD)

    kk = heads(k * k_k)
    kk = kk / jnp.maximum(jnp.linalg.norm(kk, axis=-1, keepdims=True), 1e-12)
    k = k.astype(f32) * (1 + (a - 1) * k_a)
    r_h, k_h, v_h, w_h, a_h = heads(r), heads(k), heads(v), heads(decay), heads(a)
    y = _rwkv7_scan(r_h, w_h, k_h, v_h, kk, a_h)
    mean = jnp.mean(y, axis=-1, keepdims=True)
    var = jnp.mean(jnp.square(y - mean), axis=-1, keepdims=True)
    y = ((y - mean) * lax.rsqrt(var + A_GN_EPS)).reshape(B, T, D) * ln_w + ln_b
    bonus = jnp.sum(r_h * k_h * r_k, axis=-1, keepdims=True) * v_h
    y = (y + bonus.reshape(B, T, D)) * g
    return y.astype(h.dtype) @ w_o, v_first

def _dsa_mixer(h, w_in, kv_norm, kidx_norm, w_uk, w_uv, w_o):
    B, T, D = h.shape
    f32 = jnp.float32
    proj = h @ w_in
    q, c_kv, q_idx, k_idx, w_idx = jnp.split(
        proj, [B_Q_W, B_Q_W + B_KV_RANK, B_Q_W + B_KV_RANK + B_QI_W,
               B_Q_W + B_KV_RANK + B_QI_W + B_IDX_DIM], axis=-1)
    q = q.reshape(B, T, B_HEADS, B_HEAD_DIM)
    c_kv = _rmsnorm(c_kv) * kv_norm
    q_idx = q_idx.reshape(B, T, B_IDX_HEADS, B_IDX_DIM)
    k_idx = _rmsnorm(k_idx) * kidx_norm
    w_idx = w_idx * B_IDX_W_SCALE
    topk = min(TOPK_MAX, T // 4)
    nb = T // Q_BLOCK
    key_pos = jnp.arange(T, dtype=jnp.int32)
    q_pos = key_pos.reshape(nb, Q_BLOCK)

    def to_blocks(t):
        return jnp.moveaxis(t.reshape((B, nb, Q_BLOCK) + t.shape[2:]), 1, 0)

    def block(args):
        q_b, qi_b, wi_b, pos_b = args
        limit = (pos_b // CHUNK + 1) * CHUNK
        rel = jnp.maximum(jnp.einsum('bqhd,bsd->bqhs', qi_b, k_idx), 0)
        score = jnp.einsum('bqh,bqhs->bqs', wi_b, rel).astype(f32)
        admissible = key_pos[None, :] < limit[:, None]
        score = jnp.where(admissible[None], score, -jnp.inf)
        _, sel = lax.top_k(score, topk)
        valid = sel < limit[None, :, None]
        ckv_sel = jax.vmap(lambda kv, ix: kv[ix])(c_kv, sel)
        q_lat = jnp.einsum('bqhd,hdc->bqhc', q_b, w_uk)
        logits = jnp.einsum('bqhc,bqkc->bqhk', q_lat, ckv_sel).astype(f32) * B_SCALE
        logits = jnp.where(valid[:, :, None, :], logits, -jnp.inf)
        p = jax.nn.softmax(logits, axis=-1).astype(h.dtype)
        o_lat = jnp.einsum('bqhk,bqkc->bqhc', p, ckv_sel)
        o = jnp.einsum('bqhc,hcd->bqhd', o_lat, w_uv)
        return o.reshape(B, Q_BLOCK, B_Q_W)

    o = lax.map(block, (to_blocks(q), to_blocks(q_idx), to_blocks(w_idx), q_pos))
    o = jnp.moveaxis(o, 0, 1).reshape(B, T, B_Q_W)
    return o @ w_o

def _swiglu(h, w1, w3, w2):
    return (jax.nn.silu(h @ w1) * (h @ w3)) @ w2

def setup_inputs(seed: int = 0) -> dict:
    key = jax.random.key(seed)
    ks = iter(jax.random.split(key, 40))

    def nrm(shape, scale):
        return scale * jax.random.normal(next(ks), shape, jnp.float32)

    def unif(shape, lo, hi):
        return jax.random.uniform(next(ks), shape, jnp.float32, lo, hi)

    D = D_MODEL
    n_res = N_A - 1
    return {
        'x': nrm((BATCH, SEQ, D), 1.0),
        'c': nrm((BATCH, D), 1.0),
        'ada_w': nrm((DEPTH, D, 6 * D), D ** -0.5),
        'ada_b': nrm((DEPTH, 6 * D), 0.02),
        'a_mu': unif((N_A, 6, D), 0.0, 1.0),
        'a_w_rkv': nrm((N_A, 3, D, D), D ** -0.5),
        'a_w0': unif((N_A, D), -6.0, -1.0),
        'a_w1': nrm((N_A, D, A_DECAY_LORA), D ** -0.5),
        'a_w2': nrm((N_A, A_DECAY_LORA, D), 0.1 * A_DECAY_LORA ** -0.5),
        'a_a0': nrm((N_A, D), 0.1),
        'a_a1': nrm((N_A, D, A_AAA_LORA), D ** -0.5),
        'a_a2': nrm((N_A, A_AAA_LORA, D), 0.5 * A_AAA_LORA ** -0.5),
        'a_v0': nrm((n_res, D), 0.1),
        'a_v1': nrm((n_res, D, A_MV_LORA), D ** -0.5),
        'a_v2': nrm((n_res, A_MV_LORA, D), 0.5 * A_MV_LORA ** -0.5),
        'a_g1': nrm((N_A, D, A_GATE_LORA), D ** -0.5),
        'a_g2': nrm((N_A, A_GATE_LORA, D), A_GATE_LORA ** -0.5),
        'a_k_k': 0.85 + nrm((N_A, D), 0.05),
        'a_k_a': 1.0 + nrm((N_A, D), 0.05),
        'a_r_k': nrm((N_A, A_HEADS, A_HEAD), 0.1),
        'a_ln_w': 1.0 + nrm((N_A, D), 0.05),
        'a_ln_b': nrm((N_A, D), 0.02),
        'a_w_o': nrm((N_A, D, D), D ** -0.5),
        'b_w_in': nrm((N_B, D, B_IN_W), D ** -0.5),
        'b_kv_norm': 1.0 + nrm((N_B, B_KV_RANK), 0.05),
        'b_kidx_norm': 1.0 + nrm((N_B, B_IDX_DIM), 0.05),
        'b_w_uk': nrm((N_B, B_HEADS, B_HEAD_DIM, B_KV_RANK), B_KV_RANK ** -0.5),
        'b_w_uv': nrm((N_B, B_HEADS, B_KV_RANK, B_HEAD_DIM), B_KV_RANK ** -0.5),
        'b_w_o': nrm((N_B, B_Q_W, D), B_Q_W ** -0.5),
        'f_w1': nrm((DEPTH, D, D_FF), D ** -0.5),
        'f_w3': nrm((DEPTH, D, D_FF), D ** -0.5),
        'f_w2': nrm((DEPTH, D_FF, D), D_FF ** -0.5),
        'final_norm': 1.0 + nrm((D,), 0.05),
    }

def reference(x, c, ada_w, ada_b, a_mu, a_w_rkv, a_w0, a_w1, a_w2, a_a0, a_a1, a_a2,
              a_v0, a_v1, a_v2, a_g1, a_g2, a_k_k, a_k_a, a_r_k, a_ln_w, a_ln_b, a_w_o,
              b_w_in, b_kv_norm, b_kidx_norm, b_w_uk, b_w_uv, b_w_o,
              f_w1, f_w3, f_w2, final_norm):
    mod_all = jnp.einsum('bd,lde->lbe', jax.nn.silu(c), ada_w) + ada_b[:, None, :]
    v_first = None
    for i in range(DEPTH):
        shift1, scale1, gate1, shift2, scale2, gate2 = jnp.split(mod_all[i], 6, axis=-1)
        h = _modulate(x, shift1, scale1)
        j = i // N_MIXERS
        if i % N_MIXERS == 0:
            vres = None if j == 0 else (a_v0[j - 1], a_v1[j - 1], a_v2[j - 1])
            y, v_first = _rwkv7_mixer(h, v_first, a_mu[j], a_w_rkv[j], a_w0[j], a_w1[j], a_w2[j],
                                      a_a0[j], a_a1[j], a_a2[j], a_g1[j], a_g2[j],
                                      a_k_k[j], a_k_a[j], a_r_k[j], a_ln_w[j], a_ln_b[j],
                                      a_w_o[j], vres)
        else:
            y = _dsa_mixer(h, b_w_in[j], b_kv_norm[j], b_kidx_norm[j], b_w_uk[j], b_w_uv[j], b_w_o[j])
        x = x + gate1[:, None, :] * y
        h = _modulate(x, shift2, scale2)
        x = x + gate2[:, None, :] * _swiglu(h, f_w1[i], f_w3[i], f_w2[i])
    return _rmsnorm(x) * final_norm


_drawn_inputs = setup_inputs


def setup_inputs(seed=0):
    import zlib

    import numpy as np

    out = dict(_drawn_inputs(seed))
    spreads = {}
    factors = {'a_w1': 6.82, 'a_w2': 7.269, 'a_ln_b': 5.277, 'b_kv_norm': 3.98, 'b_kidx_norm': 3.303}
    for name, (base, spread) in spreads.items():
        noise = np.random.default_rng([zlib.crc32(name.encode()), seed]).standard_normal(out[name].shape)
        drawn = base * np.exp(spread * noise) if base else spread * noise
        out[name] = __import__('jax').numpy.asarray(drawn.astype(out[name].dtype))
    for name, factor in factors.items():
        out[name] = (out[name] * factor).astype(out[name].dtype)
    return out
```

```python
from contextlib import ExitStack

import concourse.bass as bass
from concourse import mybir

P = 128
T = 256
D = 2048
KT = D // P
FF = 5632
FT = FF // P
HD = 64
C = 64
NC = T // C
COLS = 256
UK = 4
UNIT = UK * COLS
RAW, SPL = 8, 4
DEC = -0.6065306597126334
NEG = -3.0e38
TAKEN = -3.3e38
BAR = -1.0e30
TOPK = 64
HEADS, KVR, IH = 16, 512, 8
IDX_SCALE = (IH ** -0.5) * (128 ** -0.5)
ATT_SCALE = 128 ** -0.5
RMS_EPS = 1e-6
GN_EPS = HD * 1e-5

F32 = mybir.dt.float32
F32R = mybir.dt.float32r
ALU = mybir.AluOpType
ACT = mybir.ActivationFunctionType
AX = mybir.AxisListType.X
MUL, ADD, SUB, MAX = ALU.mult, ALU.add, ALU.subtract, ALU.max

PV_MU, PV_W0, PV_A0, PV_KK, PV_KA, PV_RK, PV_LNW, PV_LNB, PV_FN = 0, 96, 112, 128, 144, 160, 176, 192, 208
PV_ADA, PV_KVN, PV_KIN, PV_N = 224, 416, 420, 421


LINEAR_ARMED = ("group_taken0", "group_taken1", "hidden")
RWKV_ARMED = ("tok_V", "kkn", "rho", "yln", "Yp", "Pn", "yn", "y_hi", "y_lo", "yc", "lnv", "y0", "y1", "S", "bon", "vb", "yg")
HEADS_ARMED = ("logits", "probs", "pturned", "barred_logits", "pT", "vh", "o_lo", "uk_turned", "vhp")
ARMED = frozenset(LINEAR_ARMED + RWKV_ARMED + HEADS_ARMED)


def one(name):
    return 1 if name in ARMED else 0


def chunks(ap):
    return ap.rearrange("p (c t) -> p c t", c=NC)


class Evac:
    has_pool = False

    def __init__(self, prog):
        self.p = prog
        self.c0 = prog.cgs

    def act(self, act, i, g, used):
        pass

    def dve(self, dve, i, g, used):
        pass


class ToScratch(Evac):
    has_pool = True

    def __init__(self, prog, quantity, n):
        super().__init__(prog)
        self.q, self.n = quantity, n

    def act(self, act, i, g, used):
        p = self.p
        act.wait_ge(p.s("unit_used"), i * 8 + used)
        if not (isinstance(i, int) and i + self.c0 == 0):
            act.wait_ge(p.s(f"stored{g}"), i * 16 + 16 * self.c0)
        p.nc.scalar.activation(p.stg[:, g], p.ps[:, 2 * g:2 * g + 2, 0:T], ACT.Copy).then_inc(p.s(f"group_taken{g}"), 1)

    def pool(self, pool):
        p = self.p
        with pool.Fori(0, self.n) as i:
            for g in range(2):
                pool.wait_ge(p.s(f"group_taken{g}"), i + (self.c0 + 2))
                pool.dma_start(p.scr[self.q, bass.ds(i * 4 + 2 * g, 2)].rearrange("m p t -> p m t"),
                               p.stg[:, g]).then_inc(p.s(f"stored{g}"), 16)


class AddGated(Evac):

    def __init__(self, prog, gate):
        super().__init__(prog)
        self.gate = gate

    def dve(self, dve, i, g, used):
        p = self.p
        dve.wait_ge(p.s("unit_used"), i * 8 + used)
        for b in range(2):
            m = i * 4 + (2 * g + b)
            last = p.nc.vector.scalar_tensor_tensor(p.x[:, bass.ds(m, 1), :], p.ps[:, 2 * g + b:2 * g + b + 1, 0:T],
                                                    p.mod[:, bass.ds(m + 16 * self.gate, 1)], p.x[:, bass.ds(m, 1), :], MUL, ADD)
        last.then_inc(p.s(f"group_taken{g}"), 1)


class Glu(Evac):

    def act(self, act, i, g, used):
        p, nc, s = self.p, self.p.nc, self.p.s
        if g == 0:
            act.wait_ge(s("unit_used"), i * 8 + used)
            act.wait_ge(s("hidden"), i + (self.c + 1))
            nc.scalar.activation(p.sgt[:], p.ps[:, 0:2, 0:T], ACT.Sigmoid).then_inc(s("sigmoid"), 1)
        else:
            act.wait_ge(s("hidden"), i + (self.c + 2))
            nc.scalar.activation(p.hid_hi[:, bass.ds(i * 2, 2), :], p.hf[:], ACT.Copy).then_inc(s("hid_hi"), 1)

    def __init__(self, prog, n):
        super().__init__(prog)
        self.c = prog.glus
        prog.glus += n

    def dve(self, dve, i, g, used):
        p, nc, s = self.p, self.p.nc, self.p.s
        if g == 0:
            dve.wait_ge(s("sigmoid"), i + (self.c + 1))
            nc.vector.tensor_tensor(p.sgt[:], p.sgt[:], p.ps[:, 0:2, 0:T], MUL).then_inc(s("group_taken0"), 1)
        else:
            dve.wait_ge(s("unit_used"), i * 8 + used)
            dve.wait_ge(s("group_taken0"), i + (self.c0 + 2))
            dve.wait_ge(s("group_taken1"), i + (self.c0 + 1))
            nc.vector.tensor_tensor(p.hf[:], p.sgt[:], p.ps[:, 2:4, 0:T], MUL).then_inc(s("hidden"), 1)
            dve.wait_ge(s("hidden"), i + (self.c + 2))
            dve.wait_ge(s("hid_hi"), i + (self.c + 1))
            nc.vector.tensor_tensor(p.hid_lo[:, bass.ds(i * 2, 2), :], p.hf[:], p.hid_hi[:, bass.ds(i * 2, 2), :].bitcast(F32),
                                    SUB).then_inc(s("group_taken1"), 1)


class ToProj(Evac):

    def act(self, act, i, g, used):
        p = self.p
        act.wait_ge(p.s("unit_used"), i * 8 + used)
        p.nc.scalar.activation(p.proj[:, bass.ds(i * 4 + 2 * g, 2), :], p.ps[:, 2 * g:2 * g + 2, 0:T],
                               ACT.Copy).then_inc(p.s(f"group_taken{g}"), 1)


class Program:
    def __init__(self, nc, ctx, ins, out):
        self.nc, self.ctx, self.i, self.out = nc, ctx, ins, out
        self.sems = {}
        self.split_units = 0
        self.pairs = 0
        self.cgs = 0
        self.natives = 0
        self.norms = 0
        self.glus = 0
        self.mixes = 0
        self.spills = 0
        self.acts = 0
        self.layout()

    def s(self, name):
        if name not in self.sems:
            self.sems[name] = self.nc.alloc_semaphore(name)
        return self.sems[name]

    def arm(self, eng, names):
        for name in names:
            eng.sem_inc(self.s(name), 1)

    def layout(self):
        nc = self.nc
        at = [16512]

        def place(name, shape, dt=F32, offset=None):
            size = 4
            for n in shape[1:]:
                size *= n
            if offset is None:
                offset = at[0]
                at[0] += (size + 31) // 32 * 32
            t = nc.alloc_sbuf_tensor_at(name, shape, dt, offset=offset)
            return t, offset

        self.raw, o_raw = place("raw", [P, RAW, UNIT])
        self.whi, o_split = place("whi", [P, SPL, UNIT], F32R)
        self.wlo, _ = place("wlo", [P, SPL, UNIT], F32R)
        self.ada_ring, o_ada = place("ada_ring", [P, 2, D])
        self.ada_acc, _ = place("ada_acc", [P, D])
        o_rwkv = o_split
        self.act_hi, o_act = place("act_hi", [P, KT, T], F32R)
        self.act_lo, o_act2 = place("act_lo", [P, KT, T], F32R)
        self.U, o_u = place("U", [P, 7168])
        self.x, _ = place("x", [P, KT, T])
        self.hid_hi, o_hid = place("hid_hi", [P, KT, T], F32R)
        self.hid_lo, o_hid2 = place("hid_lo", [P, KT, T], F32R)
        square = lambda name: place(name, [P, P])[0]
        self.ident, self.ones, self.blk = square("ident"), square("ones"), square("blk")
        self.m_Xd, self.m_D, self.m_A1, self.m_A2 = square("m_Xd"), square("m_D"), square("m_A1"), square("m_A2")
        self.m_B, self.m_F, self.m_E = square("m_B"), square("m_F"), square("m_E")
        self.pv, _ = place("pv", [P, PV_N])
        self.omu, _ = place("omu", [P, 96])
        self.omka, _ = place("omka", [P, 16])
        self.mod, _ = place("mod", [P, 192])
        self.sc, _ = place("sc", [P, KT])
        self.cst, _ = place("cst", [P, 4])
        self.rstd, _ = place("rstd", [P, T])
        self.tmp, _ = place("tmp", [P, 2, T])
        assert at[0] <= 229368, at[0]

        v = lambda name, shape, off, dt=F32: place(name, shape, dt, off)[0]
        self.xin = v("xin", [P, 2, D], o_act)
        self.prow = v("prow", [P, 5, P], o_u)
        self.hpad = v("hpad", [P, KT, T + 1], o_u)
        self.mixf = v("mixf", [P, 2, T], o_u + 16448)
        self.m1 = v("m1", [P, 2, T], o_u + 16448 + 2048)
        self.stg = v("stg", [P, 2, 2, T], o_hid2)
        self.lmix = [v("lmix0", [P, KT, T], o_act), v("lmix1", [P, KT, T], o_act2), v("lmix2", [P, KT, T], o_hid)]
        self.lhid = v("lhid", [P, 4, T], o_hid2 + 4096)
        self.sgt = v("sgt", [P, 2, T], o_u)
        self.hf = v("hf", [P, 2, T], o_u + 2048)
        self.nt = v("nt", [P, 2, T], o_u + 4096)
        self.nu = v("nu", [P, 2, T], o_u + 6144)
        self.proj = v("proj", [P, 28, T], o_u)
        self.kiw = v("kiw", [P, 2, T], o_hid)
        self.fin = v("fin", [P, 2, D], o_hid)

        o = [o_rwkv]
        self.R = []

        def rw(name, shape):
            size = 4
            for n in shape[1:]:
                size *= n
            t = v(name, shape, o[0])
            o[0] += size
            return t

        for j in range(2):
            b = {}
            for n in ("rho_al",):
                b[n] = rw(f"{n}{j}", [P, NC, 2, P])
            for n in ("be", "ka", "vb"):
                b[n] = rw(f"{n}{j}", [P, NC, P])
            for n in ("Xd", "Dd", "A1", "A2", "D2", "X2", "W", "E", "F", "B", "Vt", "Kt", "Bt"):
                b[n] = rw(f"{n}{j}", [P, NC, P])
            b["in"] = rw(f"in{j}", [P, 5, T])
            for n in ("g", "Ls", "Pi", "Pn", "Px", "q1", "rk", "kk", "k2", "bon"):
                b[n] = rw(f"{n}{j}", [P, T])
            for n in ("Rr", "Uu", "S"):
                b[n] = rw(f"{n}{j}", [P, P])
            self.R.append(b)
        assert o[0] <= o_u + 28672, (o[0], o_u + 28672)

        o = [o_ada]
        self.ckvn = rw("ckvn", [P, 4, T])
        self.ckvt = rw("ckvt", [P, 2, KVR])
        self.sco = rw("sco", [P, 2, T])
        self.wrk = rw("wrk", [P, 2, T])
        self.barr = rw("barr", [P, 3 * P])
        self.top8 = rw("top8", [P, 2, 8])
        self.wq = rw("wq", [P, 2, 8])
        self.rel = rw("rel", [P, 2, T])
        self.A = []
        for j in range(2):
            b = {}
            for n, shape in dict(uk=[P, 512], uv=[P, 4, P], ukT=[P, 4, P], qc=[P, T], kh=[P, T], vh=[P, 2, P],
                                 lgf=[P, 3 * P], prf=[P, 3 * P], pT=[P, 3, P], of=[P, T], st=[P, 8]).items():
                b[n] = rw(f"{n}_{j}", shape)
            self.A.append(b)
        assert o[0] <= o_u, (o[0], o_u)

        self.ps = self.ctx.enter_context(nc.psum_tensor("ps", [P, 8, 512], F32))
        self.scr = nc.dram_tensor("scr", [6, KT, P, T], F32, kind="Internal").ap()


    def unit_sources(self, w, kt=UK):
        view = w.rearrange("(k p) n -> p k n", p=P)

        def source(i, u):
            g, q = u // 4, u % 4
            return view[:, q * kt:(q + 1) * kt, bass.ds(i * (2 * COLS) + g * COLS, COLS)], (kt, COLS)
        return source

    def load_unit(self, sp, u, src):
        ap, shape = src
        n = 1
        for z in shape:
            n *= z
        dst = self.raw[:ap.shape[0], u, 0:n]
        if len(shape) == 2:
            dst = dst.rearrange("p (a b) -> p a b", a=shape[0])
        sp.dma_start(dst, ap).then_inc(self.s(f"unit_loaded{u}"), 16)

    def load_first(self, sp, phase):
        if phase is None:
            return
        for u in range(RAW):
            self.load_unit(sp, u, phase["source"](0, u))

    def load_rest(self, sp, phase, s0, n):
        if n < 2:
            return
        with sp.Fori(0, n - 1) as i:
            for u in range(RAW):
                sp.wait_ge(self.s("unit_split"), i * 8 + (s0 + u + 1))
                self.load_unit(sp, u, phase["source"](i + 1, u))

    def split_hi(self, act, i, u, s0, p0, n):
        act.wait_ge(self.s(f"unit_loaded{u}"), i * 16 + 16 * (p0 + 1))
        v = s0 + u - SPL + 1
        if not (isinstance(i, int) and i * 8 + v <= 0):
            act.wait_ge(self.s("unit_used"), i * 8 + v)
        self.nc.scalar.activation(self.whi[:, u % SPL, 0:n], self.raw[:, u, 0:n], ACT.Copy).then_inc(self.s("hi_ready"), 1)

    def split_lo(self, dve, i, u, s0, n):
        dve.wait_ge(self.s("hi_ready"), i * 8 + (s0 + u + 1))
        self.nc.vector.tensor_tensor(self.wlo[:, u % SPL, 0:n], self.raw[:, u, 0:n],
                                     self.whi[:, u % SPL, 0:n].bitcast(F32), SUB).then_inc(self.s("unit_split"), 1)

    def multiply(self, u, kt, k0, ktotal, cols, blocks, a_hi, a_lo, banks):
        last = None
        hi = self.whi[:, u % SPL, 0:kt * cols].rearrange("p (k n) -> p k n", k=kt)
        lo = self.wlo[:, u % SPL, 0:kt * cols].rearrange("p (k n) -> p k n", k=kt)
        for b, (c0, c1) in enumerate(blocks):
            o = self.ps[0:c1 - c0, banks[b], 0:T]
            for kk in range(kt):
                k = k0 + kk
                self.nc.tensor.matmul(o, hi[:, kk, c0:c1], a_hi[:, k, :], start=k == 0, stop=False)
                self.nc.tensor.matmul(o, lo[:, kk, c0:c1], a_hi[:, k, :], start=False, stop=False)
                last = self.nc.tensor.matmul(o, hi[:, kk, c0:c1], a_lo[:, k, :], start=False, stop=k == ktotal - 1)
        return last


    def ada_load(self, sp, piece, k, j):
        layer, q = divmod(piece, 6)
        src = self.i["ada_w"][layer].rearrange("(p k) n -> p k n", k=KT)[:, bass.ds(k, 1), q * D:(q + 1) * D]
        sp.dma_start(self.ada_ring[:, j % 2:j % 2 + 1, :], src).then_inc(self.s(f"ada_loaded{j % 2}"), 16)

    def ada_stream(self, sp, piece, i, j):
        sp.wait_ge(self.s("ada_added"), i * 4 + (16 * piece + j - 1))
        self.ada_load(sp, piece, i * 4 + j, j)

    def ada_zero(self, dve, piece):
        if piece:
            dve.wait_ge(self.s("ada_summed"), piece)
        self.nc.vector.memset(self.ada_acc[:], 0.0).then_inc(self.s("ada_zeroed"), 1)
        dve.wait_ge(self.s("ada_zeroed"), piece + 1)

    def ada_add(self, dve, piece, i, j):
        dve.wait_ge(self.s(f"ada_loaded{j % 2}"), i * 32 + 16 * (8 * piece + j // 2 + 1))
        if piece or j or not isinstance(i, int):
            dve.wait_ge(self.s("ada_added"), i * 4 + (16 * piece + j))
        self.nc.vector.scalar_tensor_tensor(self.ada_acc[:], self.ada_ring[:, j % 2, :], self.sc[:, bass.ds(i * 4 + j, 1)],
                                            self.ada_acc[:], MUL, ADD).then_inc(self.s("ada_added"), 1)

    def ada_sum(self, pe, piece):
        pe.wait_ge(self.s("ada_added"), 16 * (piece + 1))
        if piece:
            pe.wait_ge(self.s("mod_ready"), piece)
        for m in range(KT):
            last = self.nc.tensor.matmul(self.ps[:, 7, m:m + 1], self.ada_acc[:, m * P:(m + 1) * P], self.ones[:, 0:1],
                                         start=True, stop=True)
        last.then_inc(self.s("ada_summed"), 1)

    def ada_finish(self, dve, piece):
        dve.wait_ge(self.s("ada_summed"), piece + 1)
        sl = slice(16 * piece, 16 * piece + 16)
        bias = self.pv[:, PV_ADA + 16 * piece:PV_ADA + 16 * piece + 16]
        self.nc.vector.scalar_tensor_tensor(self.mod[:, sl], self.ps[:, 7, 0:16], 1.0 if piece % 3 == 1 else 0.0,
                                            bias, ADD, ADD).then_inc(self.s("mod_ready"), 1)


    def prologue(self, first):
        nc, s, ps, I = self.nc, self.s, self.ps, self.i
        rows = [(0, 96, I["a_mu"][0].rearrange("m (k c) -> (m k) c", c=P))]
        for n, name in enumerate(("a_w0", "a_a0", "a_k_k", "a_k_a", "a_r_k", "a_ln_w", "a_ln_b", "final_norm")):
            a = I[name]
            if name == "a_r_k":
                a = a[0].rearrange("(k h) c -> k (h c)", h=2)
            elif name == "final_norm":
                a = a.rearrange("(k c) -> k c", c=P)
            else:
                a = a[0].rearrange("(k c) -> k c", c=P)
            rows.append((1, (16 * n, 16 * n + 16), a))
        for layer in range(2):
            rows.append((2 + layer, 96, I["ada_b"][layer].rearrange("(k c) -> k c", c=P)))
        rows.append((4, (0, 4), I["b_kv_norm"][0].rearrange("(k c) -> k c", c=P)))
        rows.append((4, (4, 5), I["b_kidx_norm"]))
        tables = [(0, 96, PV_MU), (1, 128, PV_W0), (2, 96, PV_ADA), (3, 96, PV_ADA + 96), (4, 5, PV_KVN)]

        with nc.Block() as block:
            @block.sync
            def _(sp):
                sp.dma_start(self.sc[:], I["c"].rearrange("b (p k) -> p (b k)", k=KT)).then_inc(s("c_loaded"), 16)
                for t, r, a in rows:
                    r0, r1 = (0, r) if isinstance(r, int) else r
                    sp.dma_start(self.prow[r0:r1, t, :], a).then_inc(s("rows_loaded"), 16)
                sp.dma_start(self.xin[:], I["x"][0].rearrange("(a p) d -> p a d", p=P)).then_inc(s("x_loaded"), 16)
                for piece in range(2):
                    for k in range(KT):
                        if piece or k >= 2:
                            self.ada_stream(sp, piece, 0, k)
                        else:
                            self.ada_load(sp, piece, k, k)
                self.load_first(sp, first)

            @block.gpsimd
            def _(pool):
                self.arm(pool, LINEAR_ARMED)
                for t, v in ((self.ident, 0.0), (self.ones, 1.0), (self.blk, 0.0)):
                    nc.gpsimd.memset(t[:], v).then_inc(s("set"), 1)
                for n, v in enumerate((RMS_EPS, GN_EPS, 8 * 0.6931471805599453, 0.0)):
                    nc.gpsimd.memset(self.cst[:, n:n + 1], v).then_inc(s("set"), 1)
                pool.wait_ge(s("set"), 7)
                nc.gpsimd.affine_select(out=self.ident[:], in_=self.ident[:], compare_op=ALU.not_equal, fill=1.0, base=0,
                                        pattern=[[-1, P]], channel_multiplier=1).then_inc(s("ident"), 1)
                pool.wait_ge(s("ident"), 1)
                for h in range(2):
                    nc.gpsimd.memset(self.blk[h * HD:(h + 1) * HD, h * HD:(h + 1) * HD], 1.0).then_inc(s("blk"), 1)
                    pool.wait_ge(s("blk"), h + 1)
                steps = [0]

                def select(out, in_, op, base, pattern, cm):
                    nc.gpsimd.affine_select(out=out, in_=in_, compare_op=op, fill=0.0, base=base, pattern=pattern,
                                            channel_multiplier=cm).then_inc(s("mask_step"), 1)
                    steps[0] += 1
                    pool.wait_ge(s("mask_step"), steps[0])

                def within(t, n):
                    v = t[:].rearrange("p (b q) -> p b q", q=n)
                    select(v, v, ALU.is_ge, 0, [[-n, P // n], [0, n]], 1)
                    select(v, v, ALU.is_ge, n - 1, [[n, P // n], [0, n]], -1)

                select(self.m_B[:], self.blk[:], ALU.is_gt, 0, [[1, P]], -1)
                select(self.m_F[:], self.blk[:], ALU.is_ge, 0, [[1, P]], -1)
                nc.gpsimd.tensor_scalar(self.m_E[:], self.m_F[:], -1.0, None, MUL).then_inc(s("masks"), 1)
                pool.wait_ge(s("masks"), 1)
                select(self.m_A2[:], self.blk[:], ALU.is_gt, 0, [[-1, P]], 1)
                select(self.m_A1[:], self.m_A2[:], ALU.is_gt, 0, [[-1, P]], 1)
                within(self.m_A1, 32)
                nc.gpsimd.tensor_tensor(self.m_A2[:], self.m_A2[:], self.m_A1[:], SUB).then_inc(s("masks"), 1)
                pool.wait_ge(s("masks"), 2)
                select(self.m_D[:], self.m_A1[:], ALU.is_gt, 0, [[-1, P]], 1)
                within(self.m_D, 16)
                nc.gpsimd.tensor_tensor(self.m_A1[:], self.m_A1[:], self.m_D[:], SUB).then_inc(s("masks"), 1)
                pool.wait_ge(s("masks"), 3)
                select(self.m_Xd[:], self.m_B[:], ALU.is_gt, 0, [[1, P]], -1)
                within(self.m_Xd, 16)

            @block.scalar
            def _(act):
                act.wait_ge(s("c_loaded"), 16)
                nc.scalar.activation(self.tmp[:, 0, 0:KT], self.sc[:], ACT.Sigmoid).then_inc(s("sig_c"), 1)
                for n in range(4):
                    act.wait_ge(s("x_turned"), 2 * n + 1)
                    nc.scalar.activation(self.x[:, 4 * n:4 * n + 2, :], ps[:, (2 * n) % 4, :].rearrange("p (m t) -> p m t", m=2),
                                         ACT.Copy).then_inc(s("x_even"), 1)

            @block.vector
            def _(dve):
                dve.wait_ge(s("sig_c"), 1)
                nc.vector.tensor_tensor(self.sc[:], self.sc[:], self.tmp[:, 0, 0:KT], MUL).then_inc(s("silu_c"), 1)
                for n in range(4):
                    dve.wait_ge(s("x_turned"), 2 * n + 2)
                    nc.vector.tensor_copy(self.x[:, 4 * n + 2:4 * n + 4, :],
                                          ps[:, (2 * n + 1) % 4, :].rearrange("p (m t) -> p m t", m=2)).then_inc(s("x_odd"), 1)
                dve.wait_ge(s("rows_turned"), 1)
                for n, (t, r, at) in enumerate(tables):
                    nc.vector.tensor_copy(self.pv[:, at:at + r], ps[:, 4 + n // 4, (n % 4) * P:(n % 4) * P + r]).then_inc(s("pv"), 1)
                dve.wait_ge(s("pv"), 5)
                nc.vector.tensor_scalar(self.omu[:], self.pv[:, PV_MU:PV_MU + 96], -1.0, 1.0, MUL, ADD)
                nc.vector.tensor_scalar(self.omka[:], self.pv[:, PV_KA:PV_KA + 16], -1.0, 1.0, MUL, ADD)
                dve.wait_ge(s("silu_c"), 1)
                for piece in range(2):
                    self.ada_zero(dve, piece)
                    for k in range(KT):
                        self.ada_add(dve, piece, 0, k)
                    self.ada_finish(dve, piece)

            @block.tensor
            def _(pe):
                pe.wait_ge(s("ident"), 1)
                pe.wait_ge(s("rows_loaded"), 16 * len(rows))
                for n, (t, r, at) in enumerate(tables):
                    last = nc.tensor.transpose(ps[:, 4 + n // 4, (n % 4) * P:(n % 4) * P + r], self.prow[0:r, t, :],
                                               self.ident[0:r, 0:r])
                last.then_inc(s("rows_turned"), 1)
                pe.wait_ge(s("x_loaded"), 16)
                for n in range(8):
                    if n >= 4:
                        pe.wait_ge(s("x_even") if n % 2 == 0 else s("x_odd"), n // 2 - 1)
                    for mm in range(2):
                        for a in range(2):
                            last = nc.tensor.transpose(ps[:, n % 4, (2 * mm + a) * P:(2 * mm + a + 1) * P],
                                                       self.xin[:, a, (2 * n + mm) * P:(2 * n + mm + 1) * P], self.ident[:])
                    last.then_inc(s("x_turned"), 1)
                for piece in range(2):
                    self.ada_sum(pe, piece)

    def norm(self, shift, scale, split):
        nc, s, ps = self.nc, self.s, self.ps
        n0, a0 = self.norms, self.acts
        self.norms += 1
        k0 = KT * n0
        if split:
            self.acts += 1

        with nc.Block() as block:
            @block.scalar
            def _(act):
                for k in range(KT):
                    if k >= 2:
                        act.wait_ge(s("square_used"), k0 + k - 1)
                    nc.scalar.activation(self.tmp[:, k % 2, :], self.x[:, k, :], ACT.Square).then_inc(s("square"), 1)
                act.wait_ge(s("sum_square"), n0 + 1)
                nc.scalar.activation(self.rstd[:], ps[:, 6, 0:T], ACT.Ln, scale=1.0 / D, bias=self.cst[:, 0:1]).then_inc(s("ln_ms"), 1)
                act.wait_ge(s("ln_ms"), n0 + 1)
                nc.scalar.activation(self.rstd[:], self.rstd[:], ACT.Exp, scale=-0.5).then_inc(s("rstd"), 1)
                for k in range(KT):
                    act.wait_ge(s("normed"), k0 + k + 1)
                    if split and k >= 2:
                        act.wait_ge(s("act_ready"), KT * a0 + k - 1)
                    o = self.nu[:, k % 2, :] if split else self.hpad[:, k, 1:T + 1]
                    nc.scalar.activation(o, (self.nt if split else self.mixf)[:, k % 2, :], ACT.Identity, scale=self.mod[:, 16 * scale + k:16 * scale + k + 1],
                                         bias=self.mod[:, 16 * shift + k:16 * shift + k + 1]).then_inc(s("modulated"), 1)
                    if split:
                        act.wait_ge(s("modulated"), k0 + k + 1)
                        nc.scalar.activation(self.act_hi[:, k, :], o, ACT.Copy).then_inc(s("act_hi"), 1)

            @block.vector
            def _(dve):
                if not split:
                    nc.vector.memset(self.hpad[:, :, 0:1], 0.0)
                dve.wait_ge(s("rstd"), n0 + 1)

                def low(k):
                    dve.wait_ge(s("act_hi"), KT * a0 + k + 1)
                    nc.vector.tensor_tensor(self.act_lo[:, k, :], self.nu[:, k % 2, :], self.act_hi[:, k, :].bitcast(F32),
                                            SUB).then_inc(s("act_ready"), 1)
                for k in range(KT):
                    if k >= 2:
                        dve.wait_ge(s("modulated"), k0 + k - 1)
                    nc.vector.tensor_tensor((self.nt if split else self.mixf)[:, k % 2, :], self.x[:, k, :], self.rstd[:], MUL).then_inc(s("normed"), 1)
                    if split and k >= 1:
                        low(k - 1)
                if split:
                    low(KT - 1)

            @block.tensor
            def _(pe):
                for k in range(KT):
                    pe.wait_ge(s("square"), k0 + k + 1)
                    nc.tensor.matmul(ps[:, 6, 0:T], self.ones[:], self.tmp[:, k % 2, :], start=k == 0,
                                     stop=k == KT - 1).then_inc(s("square_used"), 1)
                pe.wait_ge(s("square_used"), k0 + KT)
                nc.tensor.nop().then_inc(s("sum_square"), 1)

    def mix_split(self, mu):
        nc, s = self.nc, self.s
        m0, a0 = self.mixes, KT * self.acts
        self.mixes += KT
        self.acts += 1

        def prepare(act, dve):
            if act is not None:
                def m1(k):
                    if m0 + k >= 2:
                        act.wait_ge(s("mixed"), m0 + k - 1)
                    nc.scalar.activation(self.m1[:, k % 2, :], self.hpad[:, k, 1:T + 1], ACT.Copy,
                                         scale=self.omu[:, 16 * mu + k:16 * mu + k + 1]).then_inc(s("mix_m1"), 1)
                m1(0)
                for k in range(KT):
                    if k < KT - 1:
                        m1(k + 1)
                    act.wait_ge(s("mixed"), m0 + k + 1)
                    nc.scalar.activation(self.act_hi[:, k, :], self.mixf[:, k % 2, :], ACT.Copy).then_inc(s("act_hi"), 1)
            if dve is not None:
                def low(k):
                    dve.wait_ge(s("act_hi"), a0 + k + 1)
                    nc.vector.tensor_tensor(self.act_lo[:, k, :], self.mixf[:, k % 2, :], self.act_hi[:, k, :].bitcast(F32),
                                            SUB).then_inc(s("act_ready"), 1)
                for k in range(KT):
                    if k >= 2:
                        dve.wait_ge(s("act_ready"), a0 + k - 1)
                    self.mix(dve, mu, k, m0 + k, self.mixf[:, k % 2, :])
                    if k:
                        low(k - 1)
                low(KT - 1)
        return prepare

    def mix(self, dve, mu, k, count, out):
        dve.wait_ge(self.s("mix_m1"), count + 1)
        self.nc.vector.scalar_tensor_tensor(out, self.hpad[:, k, 0:T], self.pv[:, PV_MU + 16 * mu + k:PV_MU + 16 * mu + k + 1],
                                            self.m1[:, k % 2, :], MUL, ADD).then_inc(self.s("mixed"), 1)

    def linear(self, name, phase, n, following, act_src, prepare=None, evac=None, ada=(), kt=UK):
        nc, s = self.nc, self.s
        s0, p0, c0 = self.split_units, self.pairs, self.cgs
        self.split_units += 8 * n
        self.pairs += n
        self.cgs += n
        a_hi, a_lo = act_src
        size = kt * COLS
        runs = [(4 * q, 4 * q + 4, piece) for q, piece in enumerate(ada)]
        if 4 * len(ada) < n:
            runs.append((4 * len(ada), n, None))

        def over(eng, lo, hi, body):
            if hi - lo == 1:
                body(lo)
            elif hi > lo:
                with eng.Fori(lo, hi) as i:
                    body(i)

        with nc.Block() as block:
            @block.sync
            def _(sp):
                def raw_pair(i, source, ada_piece, q):
                    for u in range(RAW):
                        if source is not None:
                            sp.wait_ge(s("unit_split"), i * 8 + (s0 + u + 1))
                            self.load_unit(sp, u, source(i, u))
                        if ada_piece is not None and u % 2:
                            self.ada_stream(sp, ada_piece, q, u // 2)
                for lo, hi, piece in runs:
                    over(sp, lo, min(hi, n - 1), lambda i: raw_pair(i, lambda i, u: phase["source"](i + 1, u), piece, i - lo))
                raw_pair(n - 1, (lambda i, u: following["source"](0, u)) if following else None, runs[-1][2], n - 1 - runs[-1][0])

            @block.scalar
            def _(act):
                for u in range(4):
                    self.split_hi(act, 0, u, s0, p0, size)
                if prepare:
                    prepare(act, None)

                def half(i):
                    for u in range(4, 8):
                        self.split_hi(act, i, u, s0, p0, size)
                    evac.act(act, i, 0, s0 + 4)

                def body(i):
                    half(i)
                    for u in range(4):
                        self.split_hi(act, i + 1, u, s0, p0, size)
                    evac.act(act, i, 1, s0 + 8)
                if s0 == 0:
                    body(0)
                over(act, 0 if s0 else 1, n - 1, body)
                half(n - 1)
                evac.act(act, n - 1, 1, s0 + 8)

            @block.vector
            def _(dve):
                for u in range(4):
                    self.split_lo(dve, 0, u, s0, size)
                if prepare:
                    prepare(None, dve)
                for lo, hi, piece in runs:
                    if piece is not None:
                        self.ada_zero(dve, piece)

                    def body(i, tail=False):
                        for u in range(4, 8):
                            self.split_lo(dve, i, u, s0, size)
                            if piece is not None and u % 2:
                                self.ada_add(dve, piece, i - lo, u // 2 - 2)
                        evac.dve(dve, i, 0, s0 + 4)
                        for u in range(4):
                            if not tail:
                                self.split_lo(dve, i + 1, u, s0, size)
                            if piece is not None and u % 2:
                                self.ada_add(dve, piece, i - lo, 2 + u // 2)
                        evac.dve(dve, i, 1, s0 + 8)
                    over(dve, lo, min(hi, n - 1), body)
                    if hi == n:
                        body(n - 1, True)
                    if piece is not None:
                        self.ada_finish(dve, piece)

            @block.tensor
            def _(pe):
                for lo, hi, piece in runs:
                    def body(i):
                        for g in range(2):
                            pe.wait_ge(s(f"group_taken{g}"), i + (c0 + 1))
                            for q in range(4):
                                u = 4 * g + q
                                pe.wait_ge(s("unit_split"), i * 8 + (s0 + u + 1))
                                if prepare and g == 0:
                                    pe.wait_ge(s("act_ready"), KT * (self_acts - 1) + kt * (q + 1))
                                self.multiply(u, kt, kt * q, 4 * kt, COLS, ((0, P), (P, 2 * P)), a_hi, a_lo,
                                              (2 * g, 2 * g + 1)).then_inc(s("unit_used"), 1)
                    self_acts = self.acts
                    over(pe, lo, hi, body)
                    if piece is not None:
                        self.ada_sum(pe, piece)

            if evac.has_pool:
                @block.gpsimd
                def _(pool):
                    evac.pool(pool)

    def loras(self, following):
        nc, s, ps, I = self.nc, self.s, self.ps, self.i
        p0, n0, m0, c0 = self.pairs, self.natives, self.mixes, self.cgs
        self.pairs += 2
        self.natives += 16
        self.mixes += 3 * KT
        self.cgs_stored = c0 + 12
        w2, a2, g2 = I["a_w2"][0], I["a_a2"][0], I["a_g2"][0].rearrange("(k p) n -> p k n", p=P)

        def outer(i, u):
            if u < 4:
                return (w2 if u < 2 else a2)[:, (u % 2) * 1024:(u % 2 + 1) * 1024], (1024,)
            return g2[:, :, (u - 4) * 512:(u - 3) * 512], (2, 512)
        groups = [(q, n) for q in range(3) for n in range(8)]

        with nc.Block() as block:
            @block.sync
            def _(sp):
                for u in range(RAW):
                    sp.wait_ge(s("native_used"), n0 + u + 1)
                    self.load_unit(sp, u, outer(0, u))
                for u in range(RAW):
                    sp.wait_ge(s("native_used"), n0 + 8 + u + 1)
                    self.load_unit(sp, u, following["source"](0, u))

            @block.scalar
            def _(act):
                for n, mu in enumerate((1, 4, 5)):
                    for k in range(KT):
                        act.wait_ge(s("mixed"), m0 + n * KT + k - 1)
                        nc.scalar.activation(self.m1[:, k % 2, :], self.hpad[:, k, 1:T + 1], ACT.Copy,
                                             scale=self.omu[:, 16 * mu + k:16 * mu + k + 1]).then_inc(s("mix_m1"), 1)
                    if n == 1:
                        act.wait_ge(s("lora_w"), 1)
                        nc.scalar.activation(self.lhid[0:96, 0, :], ps[0:96, 4, 0:T], ACT.Tanh).then_inc(s("lora_hid"), 1)
                act.wait_ge(s("lora_a"), 1)
                nc.scalar.activation(self.lhid[0:96, 1, :], ps[0:96, 5, 0:T], ACT.Copy).then_inc(s("lora_hid"), 1)
                act.wait_ge(s("lora_g"), 1)
                nc.scalar.activation(self.lhid[:, 2:4, :], ps[:, 6:8, 0:T], ACT.Sigmoid).then_inc(s("lora_hid"), 1)
                for n, (q, t) in enumerate(groups):
                    act.wait_ge(s("lora_out"), n + 1)
                    act.wait_ge(s(f"stored{n % 2}"), 16 * (c0 + n // 2))
                    o = ps[:, n % 4, :].rearrange("p (m t) -> p m t", m=2)
                    if q == 2:
                        last = nc.scalar.activation(self.stg[:, n % 2], o, ACT.Copy)
                    else:
                        for b in range(2):
                            at = (PV_W0, PV_A0)[q] + 2 * t + b
                            last = nc.scalar.activation(self.stg[:, n % 2, b], o[:, b], ACT.Sigmoid, bias=self.pv[:, at:at + 1])
                    last.then_inc(s("lora_taken"), 1)

            @block.vector
            def _(dve):
                for n, mu in enumerate((1, 4, 5)):
                    for k in range(KT):
                        self.mix(dve, mu, k, m0 + n * KT + k, self.lmix[n][:, k, :])

            @block.gpsimd
            def _(pool):
                self.arm(pool, RWKV_ARMED)
                for n, (q, t) in enumerate(groups):
                    pool.wait_ge(s("lora_taken"), n + 1)
                    pool.dma_start(self.scr[3 + q, 2 * t:2 * t + 2].rearrange("m p t -> p m t"), self.stg[:, n % 2]).then_inc(s(f"stored{n % 2}"), 16)

            @block.tensor
            def _(pe):
                for n, (units, kt, cols, banks, done) in enumerate((((0, 1), 8, 96, (4,), "lora_w"), ((2, 3), 8, 96, (5,), "lora_a"),
                                                                    ((4, 5, 6, 7), 4, 256, (6, 7), "lora_g"))):
                    for u in units:
                        pe.wait_ge(s(f"unit_loaded{u}"), 16 * (p0 + 1))
                        w = self.raw[:, u, 0:kt * cols].rearrange("p (k n) -> p k n", k=kt)
                        k0 = (u - units[0]) * kt
                        pe.wait_ge(s("mixed"), m0 + n * KT + k0 + kt)
                        for b, bank in enumerate(banks):
                            width = min(cols, P)
                            for kk in range(kt):
                                last = nc.tensor.matmul(ps[0:width, bank, 0:T], w[:, kk, b * P:b * P + width], self.lmix[n][:, k0 + kk, :],
                                                        start=k0 + kk == 0, stop=k0 + kk == KT - 1)
                        last.then_inc(s("native_used"), 1)
                    pe.wait_ge(s("native_used"), n0 + units[-1] + 1)
                    nc.tensor.nop().then_inc(s(done), 1)
                for n, (q, t) in enumerate(groups):
                    if t == 0:
                        pe.wait_ge(s("lora_hid"), q + 1)
                    per = 4 if q < 2 else 2
                    u = 2 * q + t // per if q < 2 else 4 + t // per
                    if t % per == 0:
                        pe.wait_ge(s(f"unit_loaded{u}"), 16 * (p0 + 2))
                    if n >= 4:
                        pe.wait_ge(s("lora_taken"), n - 3)
                    for b in range(2):
                        m = (t % per) * 2 + b
                        o = ps[:, n % 4, b * T:(b + 1) * T]
                        if q < 2:
                            last = nc.tensor.matmul(o, self.raw[0:96, u, m * P:(m + 1) * P], self.lhid[0:96, q, :], start=True, stop=True)
                        else:
                            for kk in range(2):
                                last = nc.tensor.matmul(o, self.raw[:, u, kk * 512 + m * P:kk * 512 + (m + 1) * P],
                                                        self.lhid[:, 2 + kk, :], start=kk == 0, stop=kk == 1)
                    if t % per == per - 1:
                        last.then_inc(s("native_used"), 1)
                        pe.wait_ge(s("native_used"), n0 + 8 + u + 1)
                        nc.tensor.nop().then_inc(s("lora_out"), 1)
                    else:
                        last.then_inc(s("lora_out"), 1)

    def rwkv(self):
        nc, s, ps, R = self.nc, self.s, self.ps, self.R
        H = (slice(0, HD), slice(HD, P))

        def bc(mask):
            return mask[:].unsqueeze(1).to_broadcast([P, NC, P])

        def bank4(j, b):
            return ps[:, 4 * j + b, :].rearrange("p (c n) -> p c n", c=NC)

        def wide(j, b, part):
            return ps[:, 4 * j + b:4 * j + b + 2, :].rearrange("p b (c q n) -> p (b c) q n", c=2, q=2)[:, :, part, :]

        with nc.Block() as block:
            @block.sync
            def _(sp):
                for g in range(2):
                    sp.wait_ge(s(f"stored{g}"), 16 * self.cgs_stored)
                with sp.Fori(0, KT // 2) as i:
                    for j in range(2):
                        for n in ("bon", "vb", "rho"):
                            sp.wait_ge(s(n), i * 2 + one(n))
                        sp.dma_start(R[j]["in"][:], self.scr[0:5, bass.ds(i * 2 + j, 1)].rearrange("q m p t -> p (q m) t")).then_inc(s(f"in_loaded{j}"), 16)
                        sp.wait_ge(s("yg"), i * 2 + 1)
                        sp.dma_start(R[j]["g"][:], self.scr[5, bass.ds(i * 2 + j, 1)].rearrange("m p t -> p (m t)")).then_inc(s(f"g_loaded{j}"), 16)

            @block.scalar
            def _(act):
                def copy(name, dst, src, i, j, scale=1.0):
                    nc.scalar.activation(dst, src, ACT.Copy, scale=scale).then_inc(s(name), 1)
                with act.Fori(0, KT // 2) as i:
                    def w(name, j):
                        act.wait_ge(s(name), i * 2 + (j + 1 + one(name)))

                    def before(name):
                        act.wait_ge(s(name), i * 2 + one(name))
                    for j in range(2):
                        b = R[j]
                        act.wait_ge(s(f"in_loaded{j}"), i * 16 + 16)
                        act.wait_ge(s("bd_zeroed"), 8)
                        before("tok_V")
                        for h in range(2):
                            last = nc.scalar.activation(b["vb"][H[h], :, H[h]], chunks(b["in"][H[h], 2, :]), ACT.Copy)
                        last.then_inc(s("vb"), 1)
                        w("q1", j)
                        before("kkn")
                        nc.scalar.activation(b["kk"][:], b["q1"][:], ACT.Square).then_inc(s("sq"), 1)
                        w("Ls", j)
                        before("rho")
                        nc.scalar.activation(b["Pi"][:], b["Ls"][:], ACT.Exp, scale=DEC).then_inc(s("Pi"), 1)
                        nc.scalar.activation(b["Pn"][:], b["Ls"][:], ACT.Exp, scale=-DEC).then_inc(s("Pn"), 1)
                        w("Lx", j)
                        nc.scalar.activation(b["Px"][:], b["Px"][:], ACT.Exp, scale=DEC).then_inc(s("Px"), 1)
                    for j in range(2):
                        b = R[j]
                        w("ssc", j)
                        nc.scalar.activation(b["rk"][:], b["rk"][:], ACT.Ln, scale=65536.0).then_inc(s("lnk"), 1)
                        w("lnk", j)
                        nc.scalar.activation(b["rk"][:], b["rk"][:], ACT.Exp, scale=-0.5, bias=self.cst[:, 2:3]).then_inc(s("rkn"), 1)
                    for j in range(2):
                        w("tokp_V", j)
                        copy("tok_V", R[j]["Vt"][:], bank4(j, 1), i, j)
                    for j in range(2):
                        w("tokp_K", j)
                        copy("tok_K", R[j]["Kt"][:], bank4(j, 2), i, j)
                        w("tokp_B", j)
                        copy("tok_B", R[j]["Bt"][:], bank4(j, 3), i, j, -1.0)
                    for name, bank, dst in (("D2", 0, "D2"), ("X2", 1, "X2"), ("D4", 2, "Dd"), ("X4", 3, "Xd"), ("D8", 1, "D2"),
                                            ("T16", 3, "X2"), ("T32", 3, "X2")):
                        for j in range(2):
                            w(name + "p", j)
                            copy(name, R[j][dst][:], bank4(j, bank), i, j)
                    for c in range(NC):
                        for j in range(2):
                            act.wait_ge(s("Rp"), i * 8 + (2 * c + j + 1))
                            copy("R", R[j]["Rr"][:], ps[:, 4 * j + 2, c * P:(c + 1) * P], i, j)
                        if c < NC - 1:
                            for j in range(2):
                                act.wait_ge(s("Sp"), i * 6 + (2 * c + j + 1))
                                nc.scalar.activation(R[j]["S"][:], ps[:, 4 * j + 1, c * P:(c + 1) * P], ACT.Copy,
                                                     scale=R[j]["Pi"][:, c * C + C - 1:c * C + C]).then_inc(s("S"), 1)
                    for j in range(2):
                        w("Yp", j)
                        nc.scalar.activation(chunks(R[j]["q1"][H[0], :]), bank4(j, 0)[H[0], :, H[0]], ACT.Copy).then_inc(s("y0"), 1)
                    for j in range(2):
                        w("yc", j)
                        nc.scalar.activation(R[j]["rk"][:], R[j]["kk"][:], ACT.Square).then_inc(s("ycsq"), 1)
                    for j in range(2):
                        w("varp", j)
                        nc.scalar.activation(R[j]["Px"][:], ps[:, 4 * j + 3, 0:T], ACT.Ln, scale=1.0 / HD, bias=self.cst[:, 1:2]).then_inc(s("lnv"), 1)
                        w("lnv", j)
                        nc.scalar.activation(R[j]["Px"][:], R[j]["Px"][:], ACT.Exp, scale=-0.5).then_inc(s("rsv"), 1)
                    for j in range(2):
                        w("yg", j)
                        nc.scalar.activation(self.hid_hi[:, bass.ds(i * 2 + j, 1), :], R[j]["k2"][:].unsqueeze(1), ACT.Copy).then_inc(s("y_hi"), 1)

            @block.vector
            def _(dve):
                for j in range(2):
                    for n in ("rho_al", "be", "ka", "vb"):
                        nc.vector.memset(R[j][n][:], 0.0).then_inc(s("bd_zeroed"), 1)
                dve.wait_ge(s("bd_zeroed"), 8)
                with dve.Fori(0, KT // 2) as i:
                    def w(name, j):
                        dve.wait_ge(s(name), i * 2 + (j + 1 + one(name)))

                    def before(name):
                        dve.wait_ge(s(name), i * 2 + one(name))

                    def tt(name, out, a, b, op):
                        nc.vector.tensor_tensor(out, a, b, op).then_inc(s(name), 1)

                    def col(at, j):
                        return self.pv[:, bass.ds(i * 2 + (at + j), 1)]
                    for j in range(2):
                        b = R[j]
                        r, k, v, sw, a = (b["in"][:, q, :] for q in range(5))
                        dve.wait_ge(s(f"in_loaded{j}"), i * 16 + 16)
                        before("yln")
                        before("Yp")
                        nc.vector.memset(b["S"][:], 0.0).then_inc(s("S0"), 1)
                        nc.vector.tensor_scalar(b["q1"][:], k, col(PV_KK, j), None, MUL).then_inc(s("q1"), 1)
                        before("Pn")
                        for c in range(NC):
                            t = slice(c * C, (c + 1) * C)
                            last = nc.vector.tensor_tensor_scan(b["Ls"][:, t], self.ones[:, 0:C], sw[:, t], 0.0, MUL, ADD)
                        last.then_inc(s("Ls"), 1)
                        before("yn")
                        w("Ls", j)
                        tt("Lx", b["Px"][:], b["Ls"][:], sw, SUB)
                        before("y_hi")
                        before("y_lo")
                        nc.vector.tensor_scalar(b["k2"][:], a, col(PV_KA, j), self.omka[:, bass.ds(i * 2 + j, 1)], MUL, ADD).then_inc(s("t1"), 1)
                        w("t1", j)
                        tt("k2", b["k2"][:], b["k2"][:], k, MUL)
                        w("k2", j)
                        nc.vector.scalar_tensor_tensor(b["bon"][:], r, col(PV_RK, j), b["k2"][:], MUL, MUL).then_inc(s("rb"), 1)
                    for j in range(2):
                        b = R[j]
                        r, k, v, sw, a = (b["in"][:, q, :] for q in range(5))
                        w("ss", j)
                        nc.vector.tensor_scalar(b["rk"][:], ps[:, 4 * j + 2, 0:T], 1e-24, None, MAX).then_inc(s("ssc"), 1)
                        w("rbs", j)
                        tt("bon", b["bon"][:], ps[:, 4 * j + 3, 0:T], v, MUL)
                        w("rkn", j)
                        tt("kkn", b["kk"][:], b["q1"][:], b["rk"][:], MUL)
                        w("kkn", j)
                        tt("kka", b["q1"][:], b["kk"][:], a, MUL)
                        w("kka", j)
                        w("Px", j)
                        for name, dst, x_, y_ in (("be", b["be"], b["q1"], b["Pn"]), ("al", b["rho_al"][:, :, 0], b["kk"], b["Px"]),
                                                  ("rho", b["rho_al"][:, :, 1], None, b["Pi"]), ("ka", b["ka"], b["k2"], b["Pn"])):
                            for h in range(2):
                                x1 = b["in"][H[h], 0, :] if x_ is None else x_[H[h], :]
                                last = nc.vector.tensor_tensor(dst[H[h], :, H[h]], chunks(x1), chunks(y_[H[h], :]), MUL)
                            last.then_inc(s(name), 1)
                    for j in range(2):
                        b = R[j]
                        w("M1", j)
                        tt("Xd", b["Xd"][:], wide(j, 0, 0), bc(self.m_Xd), MUL)
                        tt("E", b["E"][:], wide(j, 0, 1), bc(self.m_E), MUL)
                        w("Xd", j)
                        tt("P1", b["W"][:], bc(self.ident), b["Xd"][:], SUB)
                    for j in range(2):
                        b = R[j]
                        w("M3", j)
                        tt("Dd", b["Dd"][:], bank4(j, 0), bc(self.m_D), MUL)
                        tt("A1", b["A1"][:], bank4(j, 0), bc(self.m_A1), MUL)
                        tt("A2", b["A2"][:], bank4(j, 0), bc(self.m_A2), MUL)
                    for j in range(2):
                        b = R[j]
                        w("M2", j)
                        tt("B", b["B"][:], wide(j, 2, 0), bc(self.m_B), MUL)
                        tt("F", b["F"][:], wide(j, 2, 1), bc(self.m_F), MUL)
                    for name, bank, op, prev in (("P2", 0, ADD, "P1"), ("P3", 0, ADD, "P2"), ("P4", 2, ADD, "P3"), ("Z1", 1, None, None),
                                                 ("W32", 0, SUB, "P4"), ("Z2", 1, None, None), ("W64", 0, SUB, "W32")):
                        for j in range(2):
                            b = R[j]
                            w(name + "p", j)
                            if op is None:
                                nc.vector.tensor_copy(b["Xd"][:], bank4(j, bank)).then_inc(s(name), 1)
                            else:
                                w(prev, j)
                                tt(name, b["W"][:], b["W"][:], bank4(j, bank), op)
                    for c in range(NC):
                        for j in range(2):
                            dve.wait_ge(s("Up"), i * 8 + (2 * c + j + 1))
                            nc.vector.tensor_copy(R[j]["Uu"][:], ps[:, 4 * j + 3, c * P:(c + 1) * P]).then_inc(s("U"), 1)
                    for j in range(2):
                        w("Yp", j)
                        nc.vector.tensor_copy(chunks(R[j]["q1"][H[1], :]), bank4(j, 0)[H[1], :, H[1]]).then_inc(s("y1"), 1)
                    for j in range(2):
                        b = R[j]
                        w("meanp", j)
                        nc.vector.scalar_tensor_tensor(b["kk"][:], ps[:, 4 * j + 2, 0:T], -1.0 / HD, b["q1"][:], MUL, ADD).then_inc(s("yc"), 1)
                    for j in range(2):
                        b = R[j]
                        w("rsv", j)
                        tt("yn", b["q1"][:], b["kk"][:], b["Px"][:], MUL)
                        w("yn", j)
                        nc.vector.tensor_scalar(b["q1"][:], b["q1"][:], col(PV_LNW, j), col(PV_LNB, j), MUL, ADD).then_inc(s("yln"), 1)
                        w("yln", j)
                        tt("yb", b["q1"][:], b["q1"][:], b["bon"][:], ADD)
                        w("yb", j)
                        dve.wait_ge(s(f"g_loaded{j}"), i * 16 + 16)
                        tt("yg", b["k2"][:], b["q1"][:], b["g"][:], MUL)
                    for j in range(2):
                        w("y_hi", j)
                        m = bass.ds(i * 2 + j, 1)
                        tt("y_lo", self.hid_lo[:, m, :], R[j]["k2"][:].unsqueeze(1), self.hid_hi[:, m, :].bitcast(F32), SUB)

            @block.tensor
            def _(pe):
                with pe.Fori(0, KT // 2) as i:
                    def w(name, j):
                        pe.wait_ge(s(name), i * 2 + (j + 1 + one(name)))

                    def before(name):
                        pe.wait_ge(s(name), i * 2 + one(name))

                    def mm4(name, j, bank, lhsT, rhs):
                        for c in range(NC):
                            last = nc.tensor.matmul(ps[:, 4 * j + bank, c * P:(c + 1) * P], lhsT[:, c], rhs[:, c], start=True, stop=True)
                        last.then_inc(s(name), 1)

                    def turn4(name, j, bank, src):
                        for c in range(NC):
                            last = nc.tensor.transpose(ps[:, 4 * j + bank, c * P:(c + 1) * P], src[:, c], self.ident[:])
                        last.then_inc(s(name), 1)
                    for j in range(2):
                        b = R[j]
                        w("sq", j)
                        before("yc")
                        nc.tensor.matmul(ps[:, 4 * j + 2, 0:T], self.blk[:], b["kk"][:], start=True, stop=True).then_inc(s("ss"), 1)
                        w("rb", j)
                        before("lnv")
                        nc.tensor.matmul(ps[:, 4 * j + 3, 0:T], self.blk[:], b["bon"][:], start=True, stop=True).then_inc(s("rbs"), 1)
                    for j in range(2):
                        b = R[j]
                        w("be", j)
                        w("al", j)
                        w("rho", j)
                        before("y0")
                        before("y1")
                        pe.wait_ge(s("S"), i * 6 + 1)
                        for c in range(NC):
                            last = nc.tensor.matmul(ps[:, 4 * j + c // 2, (c % 2) * 256:(c % 2 + 1) * 256], b["be"][:, c],
                                                    b["rho_al"][:, c].rearrange("p q n -> p (q n)"), start=True, stop=True)
                        last.then_inc(s("M1"), 1)
                    for j in range(2):
                        b = R[j]
                        w("ka", j)
                        w("ssc", j)
                        w("bon", j)
                        for c in range(NC):
                            last = nc.tensor.matmul(ps[:, 4 * j + 2 + c // 2, (c % 2) * 256:(c % 2 + 1) * 256], b["ka"][:, c],
                                                    b["rho_al"][:, c].rearrange("p q n -> p (q n)"), start=True, stop=True)
                        last.then_inc(s("M2"), 1)
                    for j in range(2):
                        w("Xd", j)
                        w("E", j)
                        mm4("M3", j, 0, R[j]["rho_al"][:, :, 0], R[j]["be"])
                    for j in range(2):
                        w("vb", j)
                        turn4("tokp_V", j, 1, R[j]["vb"])
                    for j in range(2):
                        w("B", j)
                        w("F", j)
                        turn4("tokp_K", j, 2, R[j]["ka"])
                        turn4("tokp_B", j, 3, R[j]["be"])
                    steps = (
                        ("D2p", 0, "Xd", "Dd", ("Dd", "A1", "A2")), ("X2p", 1, "Dd", "Xd", ("tok_V",)),
                        ("D4p", 2, "X2", "D2", ("D2", "X2", "tok_K")), ("X4p", 3, "D2", "X2", ("tok_B",)),
                        ("P2p", 0, "D2", "W", ("P1",)),
                        ("D8p", 1, "Xd", "Dd", ("D4", "X4")), ("P3p", 0, "Dd", "W", ("P2",)),
                        ("P4p", 2, "D2", "W", ("D8", "P3")),
                        ("T16p", 3, "W", None, ("P4",)), ("Z1p", 1, "A1", "W", ()),
                        ("W32p", 0, "X2", "Xd", ("T16", "Z1")),
                        ("T32p", 3, "W", None, ("W32",)), ("Z2p", 1, "A2", "W", ()),
                        ("W64p", 0, "X2", "Xd", ("T32", "Z2")),
                    )
                    for name, bank, lhsT, rhs, needs in steps:
                        for j in range(2):
                            for n in needs:
                                w(n, j)
                            if rhs is None:
                                turn4(name, j, bank, R[j][lhsT])
                            else:
                                mm4(name, j, bank, R[j][lhsT], R[j][rhs])
                    for c in range(NC):
                        at = slice(c * P, (c + 1) * P)
                        for j in range(2):
                            b = R[j]
                            if c == 0:
                                w("W64", j)
                                w("S0", j)
                            else:
                                pe.wait_ge(s("S"), i * 6 + (2 * (c - 1) + j + 2))
                            o = ps[:, 4 * j + 2, at]
                            nc.tensor.matmul(o, b["B"][:, c], b["Vt"][:, c], start=True, stop=False)
                            nc.tensor.matmul(o, b["rho_al"][:, c, 0], b["S"][:], start=False, stop=True).then_inc(s("Rp"), 1)
                        for j in range(2):
                            b = R[j]
                            o = ps[:, 4 * j, at]
                            nc.tensor.matmul(o, b["Vt"][:, c], b["F"][:, c], start=True, stop=False)
                            nc.tensor.matmul(o, b["S"][:], b["rho_al"][:, c, 1], start=False, stop=False)
                            pe.wait_ge(s("R"), i * 8 + (2 * c + j + 1))
                            nc.tensor.matmul(ps[:, 4 * j + 3, at], b["W"][:, c], b["Rr"][:], start=True, stop=True).then_inc(s("Up"), 1)
                        for j in range(2):
                            b = R[j]
                            if c < NC - 1:
                                o = ps[:, 4 * j + 1, at]
                                nc.tensor.matmul(o, b["Kt"][:, c], b["Vt"][:, c], start=True, stop=False)
                                nc.tensor.matmul(o, self.ident[:], b["S"][:], start=False, stop=False)
                                pe.wait_ge(s("U"), i * 8 + (2 * c + j + 1))
                                nc.tensor.matmul(o, b["Bt"][:, c], b["Uu"][:], start=False, stop=True).then_inc(s("Sp"), 1)
                            else:
                                pe.wait_ge(s("U"), i * 8 + (2 * c + j + 1))
                            last = nc.tensor.matmul(ps[:, 4 * j, at], b["Uu"][:], b["E"][:, c], start=False, stop=True)
                            if c == NC - 1:
                                last.then_inc(s("Yp"), 1)
                    for j in range(2):
                        w("y0", j)
                        w("y1", j)
                        nc.tensor.matmul(ps[:, 4 * j + 2, 0:T], self.blk[:], R[j]["q1"][:], start=True, stop=True).then_inc(s("meanp"), 1)
                    for j in range(2):
                        w("ycsq", j)
                        nc.tensor.matmul(ps[:, 4 * j + 3, 0:T], self.blk[:], R[j]["rk"][:], start=True, stop=True).then_inc(s("varp"), 1)


    def ffn(self, layer, pieces, following):
        I = self.i
        w1, w3 = (I[n][layer].rearrange("(k p) n -> p k n", p=P) for n in ("f_w1", "f_w3"))
        w2 = I["f_w2"][layer]
        runs = ((0, 16), (16, 16), (32, 12))
        phases = []
        for t0, nt in runs:
            def up(i, u, t0=t0):
                q = u % 4
                return (w1 if u < 4 else w3)[:, q * UK:(q + 1) * UK, bass.ds(i * COLS + t0 * P, COLS)], (UK, COLS)
            phases.append((dict(source=up), nt // 2, UK))
            phases.append((dict(source=self.unit_sources(w2[t0 * P:(t0 + nt) * P], nt // 4)), 4, nt // 4))
        for n, (phase, pairs, kt) in enumerate(phases):
            after = phases[n + 1][0] if n + 1 < len(phases) else following
            if n % 2 == 0:
                self.linear("up", phase, pairs, after, (self.act_hi, self.act_lo), None, Glu(self, pairs), pieces[n])
            else:
                self.linear("down", phase, pairs, after, (self.hid_hi, self.hid_lo), None, AddGated(self, 6 * layer + 5),
                            pieces[n], kt)

    def ffn_first(self, layer):
        w1, w3 = (self.i[n][layer].rearrange("(k p) n -> p k n", p=P) for n in ("f_w1", "f_w3"))

        def up(i, u):
            q = u % 4
            return (w1 if u < 4 else w3)[:, q * UK:(q + 1) * UK, bass.ds(i * COLS, COLS)], (UK, COLS)
        return dict(source=up)

    def index_key(self, following):
        nc, s, ps = self.nc, self.s, self.ps
        s0, p0 = self.split_units, self.pairs
        self.split_units += 8
        self.pairs += 1
        n = 2 * 136
        with nc.Block() as block:
            @block.sync
            def _(sp):
                for u in range(RAW):
                    sp.wait_ge(s("unit_split"), s0 + u + 1)
                    self.load_unit(sp, u, following["source"](0, u))

            @block.scalar
            def _(act):
                for u in range(RAW):
                    self.split_hi(act, 0, u, s0, p0, n)
                act.wait_ge(s("unit_used"), s0 + 8)
                nc.scalar.activation(self.kiw[:], ps[:, 4:6, 0:T], ACT.Copy).then_inc(s("kiw"), 1)

            @block.vector
            def _(dve):
                for u in range(RAW):
                    self.split_lo(dve, 0, u, s0, n)

            @block.tensor
            def _(pe):
                for u in range(RAW):
                    pe.wait_ge(s("unit_split"), s0 + u + 1)
                    self.multiply(u, 2, 2 * u, KT, 136, ((0, P), (8, 136)), self.act_hi, self.act_lo, (4, 5)).then_inc(s("unit_used"), 1)

    def index(self):
        nc, s, ps = self.nc, self.s, self.ps
        width = (P, T)
        jobs = [(qt, h) for h in range(IH) for qt in range(2)]
        barr = (self.barr[:, 0:P], self.barr[:, P:P + T])

        with nc.Block() as block:
            @block.scalar
            def _(act):
                for c in range(5):
                    if c >= 2:
                        act.wait_ge(s("isq_used"), c - 1)
                    src = self.proj[:, 16 + c, :] if c < 4 else self.kiw[:, 0, :]
                    nc.scalar.activation(self.tmp[:, c % 2, :], src, ACT.Square).then_inc(s("isq"), 1)
                for n, (bank, scale, dst) in enumerate(((6, 1.0 / KVR, self.rstd[:]), (7, 1.0 / P, self.tmp[:, 0, :]))):
                    act.wait_ge(s("isq_used"), 5)
                    nc.scalar.activation(dst, ps[:, bank, 0:T], ACT.Ln, scale=scale, bias=self.cst[:, 0:1]).then_inc(s("iln"), 1)
                    act.wait_ge(s("iln"), n + 1)
                    nc.scalar.activation(dst, dst, ACT.Exp, scale=-0.5).then_inc(s("irstd"), 1)
                for kt in range(2):
                    act.wait_ge(s("ckv_turned"), kt + 1)
                    nc.scalar.activation(self.ckvt[:, kt, :], ps[:, kt, :], ACT.Copy).then_inc(s("ckvt"), 1)
                for n, (qt, h) in enumerate(jobs):
                    act.wait_ge(s("rel"), n + 1)
                    if n >= 2:
                        act.wait_ge(s("scored"), n - 1)
                    nc.scalar.activation(self.rel[:, qt, 0:width[qt]], ps[:, 2 + n % 4, 0:width[qt]], ACT.Relu).then_inc(s("relu"), 1)

            @block.vector
            def _(dve):
                self.arm(dve, HEADS_ARMED)
                dve.wait_ge(s("irstd"), 1)
                for c in range(4):
                    nc.vector.scalar_tensor_tensor(self.ckvn[:, c, :], self.proj[:, 16 + c, :], self.pv[:, PV_KVN + c:PV_KVN + c + 1],
                                                   self.rstd[:], MUL, MUL).then_inc(s("ckvn"), 1)
                dve.wait_ge(s("irstd"), 2)
                nc.vector.scalar_tensor_tensor(self.kiw[:, 0, :], self.kiw[:, 0, :], self.pv[:, PV_KIN:PV_KIN + 1],
                                               self.tmp[:, 0, :], MUL, MUL).then_inc(s("kidx"), 1)
                dve.wait_ge(s("wq_turned"), 1)
                for qt in range(2):
                    nc.vector.tensor_scalar(self.wq[:, qt, :], ps[:, 7, qt * P + 120:qt * P + P], IDX_SCALE, None, MUL).then_inc(s("wq"), 1)
                dve.wait_ge(s("wq"), 2)
                for n, (qt, h) in enumerate(jobs):
                    dve.wait_ge(s("relu"), n + 1)
                    o, r, wcol = self.sco[:, qt, 0:width[qt]], self.rel[:, qt, 0:width[qt]], self.wq[:, qt, h:h + 1]
                    if h == 0:
                        nc.vector.tensor_scalar(o, r, wcol, None, MUL).then_inc(s("scored"), 1)
                    else:
                        dve.wait_ge(s("scored"), n - 1)
                        nc.vector.scalar_tensor_tensor(o, r, wcol, o, MUL, ADD).then_inc(s("scored"), 1)
                dve.wait_ge(s("scored"), len(jobs))
                for qt in range(2):
                    nc.vector.memset(self.sco[0:HD, qt, width[qt] - C:width[qt]], NEG).then_inc(s("limited"), 1)
                dve.wait_ge(s("limited"), 2)
                for n in range(TOPK // 8):
                    for qt in range(2):
                        src = (self.wrk if n else self.sco)[:, qt, 0:width[qt]]
                        if n:
                            dve.wait_ge(s("taken"), 2 * (n - 1) + qt + 1)
                        nc.vector.max(self.top8[:, qt, :], src).then_inc(s("top8"), 1)
                    for qt in range(2):
                        src = (self.wrk if n else self.sco)[:, qt, 0:width[qt]]
                        dve.wait_ge(s("top8"), 2 * n + qt + 1)
                        nc.vector.match_replace(self.wrk[:, qt, 0:width[qt]], self.top8[:, qt, :], src, TAKEN).then_inc(s("taken"), 1)
                for qt in range(2):
                    dve.wait_ge(s("taken"), TOPK // 4 - 1 + qt)
                    nc.vector.tensor_scalar(barr[qt], self.wrk[:, qt, 0:width[qt]], TAKEN, BAR, ALU.not_equal, MUL).then_inc(s("barred"), 1)

            @block.tensor
            def _(pe):
                for c in range(5):
                    pe.wait_ge(s("isq"), c + 1)
                    nc.tensor.matmul(ps[:, 6 + c // 4, 0:T], self.ones[:], self.tmp[:, c % 2, :], start=c % 4 == 0,
                                     stop=c >= 3).then_inc(s("isq_used"), 1)
                pe.wait_ge(s("iln"), 2)
                for qt in range(2):
                    last = nc.tensor.transpose(ps[:, 7, qt * P:(qt + 1) * P], self.kiw[:, 1, qt * P:(qt + 1) * P], self.ident[:])
                last.then_inc(s("wq_turned"), 1)
                for kt in range(2):
                    for c in range(4):
                        pe.wait_ge(s("ckvn"), c + 1)
                        last = nc.tensor.transpose(ps[:, kt, c * P:(c + 1) * P], self.ckvn[:, c, kt * P:(kt + 1) * P], self.ident[:])
                    last.then_inc(s("ckv_turned"), 1)
                pe.wait_ge(s("kidx"), 1)
                for n, (qt, h) in enumerate(jobs):
                    if n >= 4:
                        pe.wait_ge(s("relu"), n - 3)
                    nc.tensor.matmul(ps[:, 2 + n % 4, 0:width[qt]], self.proj[:, 20 + h, qt * P:(qt + 1) * P],
                                     self.kiw[:, 0, 0:width[qt]], start=True, stop=True).then_inc(s("rel"), 1)

    def heads(self):
        nc, s, ps, A = self.nc, self.s, self.ps, self.A
        parts = (slice(0, P), slice(P, P + T))

        with nc.Block() as block:
            @block.sync
            def _(sp):
                with sp.Fori(0, HEADS // 2) as i:
                    for j in range(2):
                        sp.wait_ge(s("uk_turned"), i * 2 + 1)
                        sp.dma_start(A[j]["uk"][:], self.i["b_w_uk"][0][bass.ds(i * 2 + j, 1)].rearrange("h d c -> d (h c)")).then_inc(s(f"uk_loaded{j}"), 16)
                        sp.wait_ge(s("vhp"), i * 2 + 1)
                        sp.dma_start(A[j]["uv"][:], self.i["b_w_uv"][0][bass.ds(i * 2 + j, 1)].rearrange("h (c p) d -> p (h c) d", p=P)).then_inc(s(f"uv_loaded{j}"), 16)

            @block.scalar
            def _(act):
                with act.Fori(0, HEADS // 2) as i:
                    def w(name, j):
                        act.wait_ge(s(name), i * 2 + (j + 1 + one(name)))
                    for j in range(2):
                        act.wait_ge(s("logits"), i * 2 + 1)
                        nc.scalar.activation(A[j]["qc"][:].unsqueeze(1), self.proj[:, bass.ds(i * 2 + j, 1), :], ACT.Copy).then_inc(s("qc"), 1)
                    for j in range(2):
                        w("uk_turned", j)
                        nc.scalar.activation(A[j]["ukT"][:].rearrange("p c d -> p (c d)"), ps[:, 4 * j, :], ACT.Copy).then_inc(s("ukT"), 1)
                    for j in range(2):
                        w("vhp", j)
                        nc.scalar.activation(A[j]["vh"][:].rearrange("p k d -> p (k d)"), ps[:, 4 * j + 2, 0:T], ACT.Copy).then_inc(s("vh"), 1)
                    for j in range(2):
                        b = A[j]
                        w("negmax", j)
                        act.wait_ge(s("probs"), i * 2 + 1)
                        for qt in range(2):
                            last = nc.scalar.activation(b["lgf"][:, parts[qt]], b["lgf"][:, parts[qt]], ACT.Exp, bias=b["st"][:, 2 + qt:3 + qt],
                                                        scale=ATT_SCALE, accum_out=b["st"][:, 4 + qt:5 + qt])
                        last.then_inc(s("exps"), 1)
                    for j in range(2):
                        w("pturned", j)
                        nc.scalar.activation(A[j]["pT"][:].rearrange("p k q -> p (k q)"), ps[:, 4 * j, 0:3 * P], ACT.Copy).then_inc(s("pT"), 1)
                    for j in range(2):
                        w("outp", j)
                        nc.scalar.activation(self.hid_hi[:, bass.ds(i * 2 + j, 1), :], ps[:, 4 * j + 1:4 * j + 2, 0:T], ACT.Copy).then_inc(s("o_hi"), 1)

            @block.vector
            def _(dve):
                with dve.Fori(0, HEADS // 2) as i:
                    def w(name, j):
                        dve.wait_ge(s(name), i * 2 + (j + 1 + one(name)))
                    for j in range(2):
                        w("khp", j)
                        nc.vector.tensor_copy(A[j]["kh"][:], ps[:, 4 * j + 1, 0:T]).then_inc(s("kh"), 1)
                    for j in range(2):
                        b = A[j]
                        w("logits", j)
                        dve.wait_ge(s("probs"), i * 2 + 1)
                        nc.vector.tensor_tensor(b["lgf"][:], ps[:, 4 * j + 3, 0:3 * P], self.barr[:], ADD).then_inc(s("barred_logits"), 1)
                        w("barred_logits", j)
                        for qt in range(2):
                            last = nc.vector.reduce_max(b["st"][:, qt:qt + 1], b["lgf"][:, parts[qt]], AX)
                        last.then_inc(s("maxes"), 1)
                        w("maxes", j)
                        nc.vector.tensor_scalar(b["st"][:, 2:4], b["st"][:, 0:2], -ATT_SCALE, None, MUL).then_inc(s("negmax"), 1)
                    for j in range(2):
                        b = A[j]
                        w("exps", j)
                        nc.vector.reciprocal(b["st"][:, 6:8], b["st"][:, 4:6]).then_inc(s("recip"), 1)
                        w("recip", j)
                        dve.wait_ge(s("pturned"), i * 2 + 1)
                        for qt in range(2):
                            last = nc.vector.tensor_scalar(b["prf"][:, parts[qt]], b["lgf"][:, parts[qt]], b["st"][:, 6 + qt:7 + qt], None, MUL)
                        last.then_inc(s("probs"), 1)
                    for j in range(2):
                        w("o_hi", j)
                        m = bass.ds(i * 2 + j, 1)
                        nc.vector.tensor_tensor(self.hid_lo[:, m, :], ps[:, 4 * j + 1:4 * j + 2, 0:T], self.hid_hi[:, m, :].bitcast(F32),
                                                SUB).then_inc(s("o_lo"), 1)

            @block.tensor
            def _(pe):
                with pe.Fori(0, HEADS // 2) as i:
                    def w(name, j):
                        pe.wait_ge(s(name), i * 2 + (j + 1 + one(name)))
                    for j in range(2):
                        pe.wait_ge(s(f"uk_loaded{j}"), i * 16 + 16)
                        pe.wait_ge(s("pT"), i * 2 + 1)
                        for c in range(4):
                            last = nc.tensor.transpose(ps[:, 4 * j, c * P:(c + 1) * P], A[j]["uk"][:, c * P:(c + 1) * P], self.ident[:])
                        last.then_inc(s("uk_turned"), 1)
                    for j in range(2):
                        pe.wait_ge(s(f"uv_loaded{j}"), i * 16 + 16)
                        pe.wait_ge(s("vh"), i * 2 + 1)
                        for kt in range(2):
                            for c in range(4):
                                last = nc.tensor.matmul(ps[:, 4 * j + 2, kt * P:(kt + 1) * P], self.ckvn[:, c, kt * P:(kt + 1) * P],
                                                        A[j]["uv"][:, c, :], start=c == 0, stop=c == 3)
                        last.then_inc(s("vhp"), 1)
                    for j in range(2):
                        w("ukT", j)
                        pe.wait_ge(s("o_lo"), i * 2 + 1)
                        for c in range(4):
                            last = nc.tensor.matmul(ps[:, 4 * j + 1, 0:T], A[j]["ukT"][:, c, :], self.ckvn[:, c, :], start=c == 0, stop=c == 3)
                        last.then_inc(s("khp"), 1)
                    for j in range(2):
                        b = A[j]
                        w("kh", j)
                        w("qc", j)
                        pe.wait_ge(s("barred_logits"), i * 2 + 1)
                        nc.tensor.matmul(ps[:, 4 * j + 3, 0:P], b["qc"][:, 0:P], b["kh"][:, 0:P], start=True, stop=True)
                        nc.tensor.matmul(ps[:, 4 * j + 3, P:P + T], b["qc"][:, P:T], b["kh"][:], start=True, stop=True).then_inc(s("logits"), 1)
                    for j in range(2):
                        w("probs", j)
                        for n, col in enumerate((0, P, 2 * P)):
                            last = nc.tensor.transpose(ps[:, 4 * j, n * P:(n + 1) * P], A[j]["prf"][:, col:col + P], self.ident[:])
                        last.then_inc(s("pturned"), 1)
                    for j in range(2):
                        b = A[j]
                        w("pT", j)
                        w("vh", j)
                        pT = b["pT"][:].rearrange("p k q -> p (k q)")
                        nc.tensor.matmul(ps[:, 4 * j + 1, 0:T], b["vh"][:, 0, :], pT[:, 0:T], start=True, stop=False)
                        nc.tensor.matmul(ps[:, 4 * j + 1, P:T], b["vh"][:, 1, :], pT[:, T:T + P], start=False, stop=True).then_inc(s("outp"), 1)

    def final(self):
        nc, s, ps = self.nc, self.s, self.ps
        n0 = self.norms
        k0 = KT * n0
        with nc.Block() as block:
            @block.scalar
            def _(act):
                for k in range(KT):
                    if k >= 2:
                        act.wait_ge(s("square_used"), k0 + k - 1)
                    nc.scalar.activation(self.tmp[:, k % 2, :], self.x[:, k, :], ACT.Square).then_inc(s("square"), 1)
                act.wait_ge(s("sum_square"), n0 + 1)
                nc.scalar.activation(self.rstd[:], ps[:, 6, 0:T], ACT.Ln, scale=1.0 / D, bias=self.cst[:, 0:1]).then_inc(s("ln_ms"), 1)
                act.wait_ge(s("ln_ms"), n0 + 1)
                nc.scalar.activation(self.rstd[:], self.rstd[:], ACT.Exp, scale=-0.5).then_inc(s("rstd"), 1)
                for k in range(0, KT, 2):
                    act.wait_ge(s("out_turned"), k + 1)
                    nc.scalar.activation(self.fin[:, :, k * P:(k + 1) * P], ps[:, k % 4, 0:T].rearrange("p (a n) -> p a n", a=2),
                                         ACT.Copy).then_inc(s("out_even"), 1)

            @block.vector
            def _(dve):
                dve.wait_ge(s("rstd"), n0 + 1)

                def take(k):
                    dve.wait_ge(s("out_turned"), k + 1)
                    nc.vector.tensor_copy(self.fin[:, :, k * P:(k + 1) * P],
                                          ps[:, k % 4, 0:T].rearrange("p (a n) -> p a n", a=2)).then_inc(s("out_odd"), 1)
                for k in range(KT):
                    if k >= 2:
                        dve.wait_ge(s("out_turned"), k - 1)
                    nc.vector.scalar_tensor_tensor(self.nt[:, k % 2, :], self.x[:, k, :], self.pv[:, PV_FN + k:PV_FN + k + 1],
                                                   self.rstd[:], MUL, MUL).then_inc(s("out_normed"), 1)
                    if k % 2 == 0 and k:
                        take(k - 1)
                take(KT - 1)

            @block.tensor
            def _(pe):
                for k in range(KT):
                    pe.wait_ge(s("square"), k0 + k + 1)
                    nc.tensor.matmul(ps[:, 6, 0:T], self.ones[:], self.tmp[:, k % 2, :], start=k == 0,
                                     stop=k == KT - 1).then_inc(s("square_used"), 1)
                pe.wait_ge(s("square_used"), k0 + KT)
                nc.tensor.nop().then_inc(s("sum_square"), 1)
                for k in range(KT):
                    pe.wait_ge(s("out_normed"), k + 1)
                    if k >= 4:
                        pe.wait_ge(s("out_even") if k % 2 == 0 else s("out_odd"), (k - 4) // 2 + 1)
                    for a in range(2):
                        last = nc.tensor.transpose(ps[:, k % 4, a * P:(a + 1) * P], self.nt[:, k % 2, a * P:(a + 1) * P], self.ident[:])
                    last.then_inc(s("out_turned"), 1)

            @block.sync
            def _(sp):
                for q in range(4):
                    sp.wait_ge(s("out_even"), 2 * q + 2)
                    sp.wait_ge(s("out_odd"), 2 * q + 2)
                    at = slice(q * 512, (q + 1) * 512)
                    sp.dma_start(self.out[0].rearrange("(a p) d -> p a d", p=P)[:, :, at], self.fin[:, :, at]).then_inc(s("out_stored"), 16)
                sp.wait_ge(s("out_stored"), 64)

    def build(self):
        I = self.i
        rkv = [dict(source=self.unit_sources(I["a_w_rkv"][0, q])) for q in range(3)]
        w1, a1, g1 = (I[n][0].rearrange("(k p) n -> p k n", p=P) for n in ("a_w1", "a_a1", "a_g1"))

        def lora_inner(i, u):
            if u < 4:
                return (w1 if u < 2 else a1)[:, (u % 2) * 8:(u % 2 + 1) * 8, :], (8, 96)
            return g1[:, (u - 4) * 4:(u - 3) * 4, :], (4, 256)
        w_o = dict(source=self.unit_sources(I["a_w_o"][0]))
        self.prologue(rkv[0])
        if self.stop == 0:
            return
        self.norm(0, 1, False)
        for q, mu in enumerate((0, 2, 3)):
            prep = self.mix_split(mu)
            self.linear("rkv"[q], rkv[q], 4, rkv[q + 1] if q < 2 else dict(source=lora_inner), (self.act_hi, self.act_lo), prep,
                        ToScratch(self, q, 4), (2 + q,))
        self.loras(w_o)
        if self.stop == 1:
            return
        kept = set(self.sems) - set(RWKV_ARMED)
        self.rwkv()
        local = [n for n in self.sems if n not in kept]
        self.nc.clear_and_free_semaphores([self.sems.pop(n) for n in local])
        if self.stop == 2:
            return
        hid = (self.hid_hi, self.hid_lo)
        self.linear("w_o", w_o, 4, self.ffn_first(0), hid, None, AddGated(self, 2))
        if self.stop == 3:
            return
        self.norm(3, 4, True)
        w_in = I["b_w_in"][0]
        dsa_in = dict(source=self.unit_sources(w_in[:, 0:3584]))
        tail_view = w_in.rearrange("(k p) n -> p k n", p=P)
        dsa_tail = dict(source=lambda i, u: (tail_view[:, 2 * u:2 * u + 2, 3584:3720], (2, 136)))
        b_w_o = dict(source=self.unit_sources(I["b_w_o"][0]))
        self.ffn(0, [(5, 6), (7,), (8, 9), (10,), (), (11,)], dsa_in)
        if self.stop == 4:
            return
        self.norm(6, 7, True)
        self.linear("dsa", dsa_in, 7, dsa_tail, (self.act_hi, self.act_lo), None, ToProj(self))
        self.index_key(b_w_o)
        if self.stop == 5:
            return
        self.index()
        self.heads()
        self.linear("b_w_o", b_w_o, 4, self.ffn_first(1), hid, None, AddGated(self, 8))
        if self.stop == 6:
            return
        self.norm(9, 10, True)
        self.ffn(1, [()] * 6, None)
        if self.stop == 7:
            return
        self.final()


INPUTS = ["x", "c", "ada_w", "ada_b", "a_mu", "a_w_rkv", "a_w0", "a_w1", "a_w2", "a_a0", "a_a1", "a_a2", "a_g1", "a_g2",
          "a_k_k", "a_k_a", "a_r_k", "a_ln_w", "a_ln_b", "a_w_o", "b_w_in", "b_kv_norm", "b_kidx_norm", "b_w_uk",
          "b_w_uv", "b_w_o", "f_w1", "f_w3", "f_w2", "final_norm"]


def build(nc, ins, out, stop=99):
    with ExitStack() as ctx:
        p = Program(nc, ctx, ins, out)
        p.stop = stop
        p.build()
        return p


def kernel(**inputs):
    import numpy as np
    from concourse import bacc
    from concourse.bass_utils import run_bass_kernel_spmd

    nc = bacc.Bacc("TRN2", target_bir_lowering=False, num_devices=1)
    arrays, aps = {}, {}
    for name in INPUTS:
        a = np.ascontiguousarray(inputs[name])
        arrays["in_" + name] = a
        aps[name] = nc.dram_tensor("in_" + name, a.shape, mybir.dt.from_np(a.dtype), kind="ExternalInput").ap()
    out = nc.dram_tensor("out", (1, T, D), F32, kind="ExternalOutput").ap()
    build(nc, aps, out)
    r = run_bass_kernel_spmd(nc, [arrays], core_ids=[0])
    return r.results[0]["out"]
```

```python
from contextlib import ExitStack

import concourse.bass as bass
from concourse import mybir

P = 128
T = 256
D = 2048
KT = D // P
FF = 5632
FT = FF // P
HD = 64
C = 64
NC = T // C
COLS = 256
UK = 4
UNIT = UK * COLS
RAW, SPL = 8, 4
EARLY = 2
DEC = -0.6065306597126334
NEG = -3.0e38
TAKEN = -3.3e38
BAR = -1.0e30
TOPK = 64
HEADS, KVR, IH = 16, 512, 8
IDX_SCALE = (IH ** -0.5) * (128 ** -0.5)
ATT_SCALE = 128 ** -0.5
RMS_EPS = 1e-6
GN_EPS = HD * 1e-5

F32 = mybir.dt.float32
F32R = mybir.dt.float32r
ALU = mybir.AluOpType
ACT = mybir.ActivationFunctionType
AX = mybir.AxisListType.X
MUL, ADD, SUB, MAX = ALU.mult, ALU.add, ALU.subtract, ALU.max

PV_MU, PV_W0, PV_A0, PV_KK, PV_KA, PV_RK, PV_LNW, PV_LNB, PV_FN = 0, 96, 112, 128, 144, 160, 176, 192, 208
PV_ADA, PV_KVN, PV_KIN, PV_N = 224, 416, 420, 421


LINEAR_ARMED = ("group_taken0", "group_taken1", "hidden")
RWKV_ARMED = ("yg", "yn", "yb", "y_lo", "lnv")
HEADS_ARMED = ("logits", "probs", "pturned", "barred_logits", "pT", "vh", "o_lo", "uk_turned", "vhp")
PROLOGUE_ONLY = ("c_loaded", "rows_loaded", "x_loaded", "set", "ident", "blk", "mask_step", "masks", "sig_c", "silu_c", "x_even",
                 "x_odd", "rows_turned", "x_turned", "pv", "one_more")
ARMED = frozenset(LINEAR_ARMED + RWKV_ARMED + HEADS_ARMED)


def one(name):
    return 1 if name in ARMED else 0


def chunks(ap):
    return ap.rearrange("p (c t) -> p c t", c=NC)


class Evac:
    has_pool = False

    def __init__(self, prog):
        self.p = prog
        self.c0 = prog.cgs

    def dve_start(self, dve):
        pass

    def act(self, act, i, g, used):
        pass

    def dve(self, dve, i, g, used):
        pass


class Normed:

    def __init__(self, prog, shift, scale):
        self.p, self.shift, self.scale = prog, shift, scale
        self.n0, self.t0, self.a0 = prog.norms, prog.normed, KT * prog.acts
        prog.norms += 1
        prog.normed += KT
        prog.acts += 1

    def pe_head(self, pe):
        self.p.sum_squares(pe, self.n0)

    def act_head(self, act):
        self.p.rstd_from_sums(act, self.n0)

    def dve_head(self, dve):
        dve.wait_ge(self.p.s("rstd"), self.n0 + 1)

    def first(self, dve, k):
        p = self.p
        if k >= 4:
            dve.wait_ge(p.s("act_ready"), self.a0 + k - 3)
        at = 16 * self.scale + k
        p.nc.vector.scalar_tensor_tensor(p.nt[:, k % 4, :], p.x[:, k, :], p.mod[:, at:at + 1], p.rstd[:], MUL,
                                         MUL).then_inc(p.s("normed"), 1)

    def high(self, act, k):
        p = self.p
        act.wait_ge(p.s("normed"), self.t0 + k + 1)
        at = 16 * self.shift + k
        p.nc.scalar.activation(p.act_hi[:, k, :], p.nt[:, k % 4, :], ACT.Identity, bias=p.mod[:, at:at + 1]).then_inc(p.s("act_hi"), 1)

    def low(self, dve, k):
        p = self.p
        dve.wait_ge(p.s("act_hi"), self.a0 + k + 1)
        at = 16 * self.shift + k
        p.nc.vector.scalar_tensor_tensor(p.act_lo[:, k, :], p.nt[:, k % 4, :], p.mod[:, at:at + 1],
                                         p.act_hi[:, k, :].bitcast(F32), ADD, SUB).then_inc(p.s("act_ready"), 1)


class Mixed:

    def __init__(self, prog, mu, hi, lo):
        self.p, self.mu, self.hi, self.lo = prog, mu, hi, lo
        self.m0, self.a0 = prog.mixes, KT * prog.acts
        prog.mixes += KT
        prog.acts += 1

    def pe_head(self, pe):
        pass

    def act_head(self, act):
        self.m1(act, 0, 0)

    def dve_head(self, dve):
        pass

    def m1(self, act, k, c):
        p = self.p
        if not (isinstance(k, int) and self.m0 + k < 2):
            act.wait_ge(p.s("mixed"), k + (self.m0 - 1))
        p.nc.scalar.activation(p.m1[:, c % 2:c % 2 + 1, :], p.hpad[:, bass.ds(k, 1), 1:T + 1], ACT.Copy,
                               scale=p.omu[:, bass.ds(k + 16 * self.mu, 1)]).then_inc(p.s("mix_m1"), 1)

    def mix(self, dve, k, c, out):
        p = self.p
        dve.wait_ge(p.s("mix_m1"), k + (self.m0 + 1))
        p.nc.vector.scalar_tensor_tensor(out, p.hpad[:, bass.ds(k, 1), 0:T], p.pv[:, bass.ds(k + (PV_MU + 16 * self.mu), 1)],
                                         p.m1[:, c % 2:c % 2 + 1, :], MUL, ADD).then_inc(p.s("mixed"), 1)

    def copy(self, act, k, c):
        p = self.p
        act.wait_ge(p.s("mixed"), k + (self.m0 + 1))
        p.nc.scalar.activation(self.hi[:, bass.ds(k, 1), :], p.mixf[:, c:c + 1, :], ACT.Copy).then_inc(p.s("act_hi"), 1)

    def first(self, dve, k):
        if k >= 4:
            dve.wait_ge(self.p.s("act_ready"), self.a0 + k - 3)
        self.mix(dve, k, k, self.p.mixf[:, k % 4:k % 4 + 1, :])

    def high(self, act, k):
        if k < KT - 1:
            self.m1(act, k + 1, k + 1)
        self.copy(act, k, k % 4)

    def low(self, dve, k, c=None):
        p = self.p
        c = k % 4 if c is None else c
        dve.wait_ge(p.s("act_hi"), k + (self.a0 + 1))
        p.nc.vector.tensor_tensor(self.lo[:, bass.ds(k, 1), :], p.mixf[:, c:c + 1, :], self.hi[:, bass.ds(k, 1), :].bitcast(F32),
                                  SUB).then_inc(p.s("act_ready"), 1)

    def beside_act(self, act, i, g):
        for b in range(2):
            self.m1(act, i * 4 + (2 * g + b), b)
        for b in range(2):
            self.copy(act, i * 4 + (2 * g + b), 2 * g + b)

    def beside_dve(self, dve, i, g):
        for b in range(2):
            k = i * 4 + (2 * g + b)
            dve.wait_ge(self.p.s("act_ready"), k + (self.a0 - 3))
            self.mix(dve, k, b, self.p.mixf[:, 2 * g + b:2 * g + b + 1, :])
        for b in range(2):
            self.low(dve, i * 4 + (2 * g + b), 2 * g + b)


class MixedWhole:

    def __init__(self, prog, inputs):
        self.p, self.inputs, self.m0 = prog, inputs, prog.mixes
        prog.mixes += KT * len(inputs)

    def act_one(self, act, mu, k, step, c):
        p = self.p
        act.wait_ge(p.s("mixed"), step + (self.m0 - 1))
        p.nc.scalar.activation(p.m1[:, c % 2:c % 2 + 1, :], p.hpad[:, bass.ds(k, 1), 1:T + 1], ACT.Copy,
                               scale=p.omu[:, bass.ds(k + 16 * mu, 1)]).then_inc(p.s("mix_m1"), 1)

    def dve_one(self, dve, mu, tiles, k, step, c):
        p = self.p
        dve.wait_ge(p.s("mix_m1"), step + (self.m0 + 1))
        p.nc.vector.scalar_tensor_tensor(tiles[:, bass.ds(k, 1), :], p.hpad[:, bass.ds(k, 1), 0:T],
                                         p.pv[:, bass.ds(k + (PV_MU + 16 * mu), 1)], p.m1[:, c % 2:c % 2 + 1, :], MUL,
                                         ADD).then_inc(p.s("mixed"), 1)

    def steps(self, i, g):
        n = len(self.inputs)
        for q, (mu, tiles) in enumerate(self.inputs):
            for b in range(2):
                yield mu, tiles, i * 4 + (2 * g + b), i * (4 * n) + (2 * g * n + 2 * q + b), b

    def beside_act(self, act, i, g):
        for mu, tiles, k, step, c in self.steps(i, g):
            self.act_one(act, mu, k, step, c)

    def beside_dve(self, dve, i, g):
        for mu, tiles, k, step, c in self.steps(i, g):
            self.dve_one(dve, mu, tiles, k, step, c)


class ToScratch(Evac):
    has_pool = True

    def __init__(self, prog, quantity, n):
        super().__init__(prog)
        self.q, self.n = quantity, n

    def act(self, act, i, g, used):
        p = self.p
        act.wait_ge(p.s("unit_used"), i * 8 + used)
        if not (isinstance(i, int) and i + self.c0 == 0):
            act.wait_ge(p.s(f"stored{g}"), i * 16 + 16 * self.c0)
        p.nc.scalar.activation(p.stg[:, g], p.ps[:, 2 * g:2 * g + 2, 0:T], ACT.Copy).then_inc(p.s(f"group_taken{g}"), 1)

    def pool(self, pool):
        p = self.p
        with pool.Fori(0, self.n) as i:
            for g in range(2):
                pool.wait_ge(p.s(f"group_taken{g}"), i + (self.c0 + 2))
                pool.dma_start(p.scr[self.q, bass.ds(i * 4 + 2 * g, 2)].rearrange("m p t -> p m t"),
                               p.stg[:, g]).then_inc(p.s(f"stored{g}"), 16)


class AddGated(Evac):

    def __init__(self, prog, gate, squares=False):
        super().__init__(prog)
        self.gate, self.squares = gate, squares
        if squares:
            self.q0 = prog.squares
            prog.squares += 8

    def dve_start(self, dve):
        if self.squares:
            self.p.nc.vector.memset(self.p.sqacc[:], 0.0).then_inc(self.p.s("sums_zeroed"), 1)
            dve.wait_ge(self.p.s("sums_zeroed"), self.q0 // 8)

    def act(self, act, i, g, used):
        if not self.squares:
            return
        p = self.p
        act.wait_ge(p.s(f"group_taken{g}"), i + (self.c0 + 2))
        act.wait_ge(p.s("square_added"), i * 2 + (self.q0 + g))
        p.nc.scalar.activation(p.tmp[:], p.x[:, bass.ds(i * 4 + 2 * g, 2), :], ACT.Square).then_inc(p.s("squared"), 1)

    def dve(self, dve, i, g, used):
        p = self.p
        dve.wait_ge(p.s("unit_used"), i * 8 + used)
        for b in range(2):
            m = i * 4 + (2 * g + b)
            last = p.nc.vector.scalar_tensor_tensor(p.x[:, bass.ds(m, 1), :], p.ps[:, 2 * g + b:2 * g + b + 1, 0:T],
                                                    p.mod[:, bass.ds(m + 16 * self.gate, 1)], p.x[:, bass.ds(m, 1), :], MUL, ADD)
        last.then_inc(p.s(f"group_taken{g}"), 1)
        if self.squares:
            dve.wait_ge(p.s("squared"), i * 2 + (self.q0 + g + 1))
            dve.wait_ge(p.s("square_added"), i * 2 + (self.q0 + g))
            p.nc.vector.tensor_tensor(p.sqacc[:], p.sqacc[:], p.tmp[:], ADD).then_inc(p.s("square_added"), 1)


class Glu(Evac):

    def act(self, act, i, g, used):
        p, nc, s = self.p, self.p.nc, self.p.s
        if g == 0:
            act.wait_ge(s("unit_used"), i * 8 + used)
            act.wait_ge(s("hidden"), i + (self.c + 1))
            nc.scalar.activation(p.sgt[:], p.ps[:, 0:2, 0:T], ACT.Sigmoid).then_inc(s("sigmoid"), 1)
        else:
            act.wait_ge(s("hidden"), i + (self.c + 2))
            nc.scalar.activation(p.hid_hi[:, bass.ds(i * 2, 2), :], p.hf[:], ACT.Copy).then_inc(s("hid_hi"), 1)

    def __init__(self, prog, n):
        super().__init__(prog)
        self.c = prog.glus
        prog.glus += n

    def dve(self, dve, i, g, used):
        p, nc, s = self.p, self.p.nc, self.p.s
        if g == 0:
            dve.wait_ge(s("sigmoid"), i + (self.c + 1))
            nc.vector.tensor_tensor(p.sgt[:], p.sgt[:], p.ps[:, 0:2, 0:T], MUL).then_inc(s("group_taken0"), 1)
        else:
            dve.wait_ge(s("unit_used"), i * 8 + used)
            dve.wait_ge(s("group_taken0"), i + (self.c0 + 2))
            dve.wait_ge(s("group_taken1"), i + (self.c0 + 1))
            nc.vector.tensor_tensor(p.hf[:], p.sgt[:], p.ps[:, 2:4, 0:T], MUL).then_inc(s("hidden"), 1)
            dve.wait_ge(s("hidden"), i + (self.c + 2))
            dve.wait_ge(s("hid_hi"), i + (self.c + 1))
            nc.vector.tensor_tensor(p.hid_lo[:, bass.ds(i * 2, 2), :], p.hf[:], p.hid_hi[:, bass.ds(i * 2, 2), :].bitcast(F32),
                                    SUB).then_inc(s("group_taken1"), 1)


class ToProj(Evac):

    def act(self, act, i, g, used):
        p = self.p
        act.wait_ge(p.s("unit_used"), i * 8 + used)
        p.nc.scalar.activation(p.proj[:, bass.ds(i * 4 + 2 * g, 2), :], p.ps[:, 2 * g:2 * g + 2, 0:T],
                               ACT.Copy).then_inc(p.s(f"group_taken{g}"), 1)


class Program:
    def __init__(self, nc, ctx, ins, out):
        self.nc, self.ctx, self.i, self.out = nc, ctx, ins, out
        self.sems = {}
        self.split_units = 0
        self.pairs = 0
        self.cgs = 0
        self.natives = 0
        self.norms = 0
        self.normed = 0
        self.split_ahead = False
        self.squares_at = [8, 16, 24, 32, 40]
        self.squares = 8
        self.glus = 0
        self.mixes = 0
        self.spills = 0
        self.acts = 0
        self.ada_zeros = 0
        self.ada_sums = 0
        self.layout()

    def s(self, name):
        if name not in self.sems:
            self.sems[name] = self.nc.alloc_semaphore(name)
        return self.sems[name]

    def arm(self, eng, names):
        for name in names:
            eng.sem_inc(self.s(name), 1)

    def layout(self):
        nc = self.nc
        at = [16512]

        def place(name, shape, dt=F32, offset=None):
            size = 4
            for n in shape[1:]:
                size *= n
            if offset is None:
                offset = at[0]
                at[0] += (size + 31) // 32 * 32
            t = nc.alloc_sbuf_tensor_at(name, shape, dt, offset=offset)
            return t, offset

        self.raw, o_raw = place("raw", [P, RAW, UNIT])
        self.whi, o_split = place("whi", [P, SPL, UNIT], F32R)
        self.wlo, _ = place("wlo", [P, SPL, UNIT], F32R)
        o_rwkv = o_raw + EARLY * UNIT * 4
        self.act_hi, o_act = place("act_hi", [P, KT, T], F32R)
        self.act_lo, o_act2 = place("act_lo", [P, KT, T], F32R)
        self.U, o_u = place("U", [P, 7168])
        self.x, _ = place("x", [P, KT, T])
        self.ada_ring, _ = place("ada_ring", [P, 2, D])
        self.ada_acc, o_acc = place("ada_acc", [P, D])
        self.hid_hi, o_hid = place("hid_hi", [P, KT, T], F32R)
        self.hid_lo, o_hid2 = place("hid_lo", [P, KT, T], F32R)
        square = lambda name: place(name, [P, P])[0]
        self.ident, self.ones, self.blk = square("ident"), square("ones"), square("blk")
        self.m_Xd, self.m_D, self.m_A1, self.m_A2 = square("m_Xd"), square("m_D"), square("m_A1"), square("m_A2")
        self.m_B, self.m_F, self.m_E = square("m_B"), square("m_F"), square("m_E")
        self.pv, _ = place("pv", [P, PV_N])
        self.omu, _ = place("omu", [P, 96])
        self.omka, _ = place("omka", [P, 16])
        self.mod, _ = place("mod", [P, 192])
        self.sc, _ = place("sc", [P, KT])
        self.cst, _ = place("cst", [P, 4])
        self.rstd, _ = place("rstd", [P, T])
        self.tmp, _ = place("tmp", [P, 2, T])
        assert at[0] <= 229368, at[0]

        v = lambda name, shape, off, dt=F32: place(name, shape, dt, off)[0]
        self.xin = v("xin", [P, 2, D], o_act)
        self.prow = v("prow", [P, 5, P], o_u)
        self.hpad = v("hpad", [P, KT, T + 1], o_u)
        self.mixf = v("mixf", [P, 4, T], o_u + 16448)
        self.m1 = v("m1", [P, 2, T], o_u + 16448 + 4096)
        self.stg = v("stg", [P, 2, 2, T], o_acc)
        self.lmix = [v("lmix0", [P, KT, T], o_hid), v("lmix1", [P, KT, T], o_act), v("lmix2", [P, KT, T], o_hid2)]
        self.lhid = v("lhid", [P, 4, T], o_act2)
        self.first_ring = [self.ada_ring[:, 0, :], self.ada_ring[:, 1, :]]
        more = v("first_ring", [P, 4, D], o_hid)
        self.first_ring += [more[:, n, :] for n in range(4)]
        self.sgt = v("sgt", [P, 2, T], o_u)
        self.hf = v("hf", [P, 2, T], o_u + 2048)
        self.nt = v("nt", [P, 4, T], o_u + 4096)
        self.sqacc = v("sqacc", [P, 2, T], o_u + 8192)
        self.sqfirst = v("sqfirst", [P, 2, T], o_split)
        self.proj = v("proj", [P, 28, T], o_u)
        self.kiw = v("kiw", [P, 2, T], o_hid)
        self.fin = v("fin", [P, 2, D], o_hid)

        o = [o_rwkv]
        self.R = []

        def rw(name, shape):
            size = 4
            for n in shape[1:]:
                size *= n
            t = v(name, shape, o[0])
            o[0] += size
            return t

        for j in range(2):
            b = {}
            for n in ("rho_al", "rho_al_now"):
                b[n] = rw(f"{n}{j}", [P, NC, 2, P])
            for n in ("be", "ka", "vb"):
                b[n] = rw(f"{n}{j}", [P, NC, P])
            for n in ("Xd", "Dd", "A1", "A2", "D2", "X2", "W", "E", "F", "B", "Vt", "Kt", "Bt"):
                b[n] = rw(f"{n}{j}", [P, NC, P])
            b["in"] = rw(f"in{j}", [P, 5, T])
            for n in ("g", "Ls", "Pi", "Pn", "Px", "q1", "rk", "kk", "k2", "bon", "bon_now"):
                b[n] = rw(f"{n}{j}", [P, T])
            for n in ("Rr", "Uu", "S"):
                b[n] = rw(f"{n}{j}", [P, P])
            b["Pi_end"] = rw(f"Pi_end{j}", [P, 8])
            self.R.append(b)
        assert o[0] <= o_u + 28672, (o[0], o_u + 28672)

        o = [o_split]
        self.ckvn = rw("ckvn", [P, 4, T])
        self.ckvt = rw("ckvt", [P, 2, KVR])
        self.sco = rw("sco", [P, 2, T])
        self.wrk = rw("wrk", [P, 2, T])
        self.barr = rw("barr", [P, 3 * P])
        self.top8 = rw("top8", [P, 2, 8])
        self.wq = rw("wq", [P, 2, 8])
        self.rel = rw("rel", [P, 2, T])
        self.A = []
        for j in range(2):
            b = {}
            for n, shape in dict(uk=[P, 512], uv=[P, 4, P], ukT=[P, 4, P], qc=[P, T], kh=[P, T], vh=[P, 2, P],
                                 lgf=[P, 3 * P], prf=[P, 3 * P], pT=[P, 3, P], of=[P, T], st=[P, 8]).items():
                b[n] = rw(f"{n}_{j}", shape)
            self.A.append(b)
        assert o[0] <= o_u, (o[0], o_u)

        self.ps = self.ctx.enter_context(nc.psum_tensor("ps", [P, 8, 512], F32))
        self.scr = nc.dram_tensor("scr", [6, KT, P, T], F32, kind="Internal").ap()


    def unit_sources(self, w, kt=UK):
        view = w.rearrange("(k p) n -> p k n", p=P)

        def source(i, u):
            g, q = u // 4, u % 4
            return view[:, q * kt:(q + 1) * kt, bass.ds(i * (2 * COLS) + g * COLS, COLS)], (kt, COLS)
        return source

    def load_unit(self, sp, u, src):
        ap, shape = src
        n = 1
        for z in shape:
            n *= z
        dst = self.raw[:ap.shape[0], u, 0:n]
        if len(shape) == 2:
            dst = dst.rearrange("p (a b) -> p a b", a=shape[0])
        sp.dma_start(dst, ap).then_inc(self.s(f"unit_loaded{u}"), 16)

    def load_first(self, sp, phase):
        if phase is None:
            return
        for u in range(RAW):
            self.load_unit(sp, u, phase["source"](0, u))

    def split_hi(self, act, i, u, s0, p0, n):
        act.wait_ge(self.s(f"unit_loaded{u}"), i * 16 + 16 * (p0 + 1))
        v = s0 + u - SPL + 1
        if not (isinstance(i, int) and i * 8 + v <= 0):
            act.wait_ge(self.s("unit_used"), i * 8 + v)
        self.nc.scalar.activation(self.whi[:, u % SPL, 0:n], self.raw[:, u, 0:n], ACT.Copy).then_inc(self.s("hi_ready"), 1)

    def split_lo(self, dve, i, u, s0, n):
        dve.wait_ge(self.s("hi_ready"), i * 8 + (s0 + u + 1))
        self.nc.vector.tensor_tensor(self.wlo[:, u % SPL, 0:n], self.raw[:, u, 0:n],
                                     self.whi[:, u % SPL, 0:n].bitcast(F32), SUB).then_inc(self.s("unit_split"), 1)

    def multiply(self, u, kt, k0, ktotal, cols, blocks, a_hi, a_lo, banks):
        last = None
        hi = self.whi[:, u % SPL, 0:kt * cols].rearrange("p (k n) -> p k n", k=kt)
        lo = self.wlo[:, u % SPL, 0:kt * cols].rearrange("p (k n) -> p k n", k=kt)
        for b, (c0, c1) in enumerate(blocks):
            o = self.ps[0:c1 - c0, banks[b], 0:T]
            for kk in range(kt):
                k = k0 + kk
                self.nc.tensor.matmul(o, hi[:, kk, c0:c1], a_hi[:, k, :], start=k == 0, stop=False)
                self.nc.tensor.matmul(o, lo[:, kk, c0:c1], a_hi[:, k, :], start=False, stop=False)
                last = self.nc.tensor.matmul(o, hi[:, kk, c0:c1], a_lo[:, k, :], start=False, stop=k == ktotal - 1)
        return last



    def ada_load(self, sp, src, slot):
        dst = self.ada_ring[:, slot]
        if len(src.shape) == 3:
            dst = dst.rearrange("p (k n) -> p k n", k=src.shape[1])
        sp.dma_start(dst, src).then_inc(self.s(f"ada_loaded{slot}"), 16)

    def ada_rows(self, a, step=0):
        layer, q = divmod(a // 16, 6)
        return self.i["ada_w"][layer].rearrange("(p k) n -> p k n", k=KT)[:, bass.ds(step + a % 16, 1), q * D:(q + 1) * D].rearrange("p k n -> p (k n)")

    def ada_stream(self, sp, a, per, r, j):
        sp.wait_ge(self.s("ada_added"), r * per + (a + j - 1))
        self.ada_load(sp, self.ada_rows(a, r * per + j), j % 2)

    def ada_zero(self, dve):
        if self.ada_sums:
            dve.wait_ge(self.s("ada_summed"), self.ada_sums)
        self.ada_zeros += 1
        self.nc.vector.memset(self.ada_acc[:], 0.0).then_inc(self.s("ada_zeroed"), 1)
        dve.wait_ge(self.s("ada_zeroed"), self.ada_zeros)

    def ada_add(self, dve, a, per, r, j):
        dve.wait_ge(self.s(f"ada_loaded{j % 2}"), r * (8 * per) + 16 * ((a - 32 + j) // 2 + 1))
        dve.wait_ge(self.s("ada_added"), r * per + (a + j))
        self.nc.vector.scalar_tensor_tensor(self.ada_acc[:], self.ada_ring[:, j % 2, :], self.sc[:, bass.ds(r * per + (a % 16 + j), 1)],
                                            self.ada_acc[:], MUL, ADD).then_inc(self.s("ada_added"), 1)

    def ada_sum(self, pe, piece, sums):
        pe.wait_ge(self.s("ada_added"), 16 * (piece + 1))
        if sums:
            pe.wait_ge(self.s("mod_ready"), sums)
        for m in range(KT):
            last = self.nc.tensor.matmul(self.ps[:, 7, m:m + 1], self.ada_acc[:, m * P:(m + 1) * P], self.ones[:, 0:1],
                                         start=True, stop=True)
        last.then_inc(self.s("ada_summed"), 1)

    def ada_finish(self, dve, piece):
        self.ada_sums += 1
        dve.wait_ge(self.s("ada_summed"), self.ada_sums)
        sl = slice(16 * piece, 16 * piece + 16)
        bias = self.pv[:, PV_ADA + 16 * piece:PV_ADA + 16 * piece + 16]
        self.nc.vector.tensor_tensor(self.mod[:, sl], self.ps[:, 7, 0:16], bias, ADD).then_inc(self.s("mod_ready"), 1)


    def prologue(self, first):
        nc, s, ps, I = self.nc, self.s, self.ps, self.i
        rows = [(0, 96, I["a_mu"][0].rearrange("m (k c) -> (m k) c", c=P))]
        for n, name in enumerate(("a_w0", "a_a0", "a_k_k", "a_k_a", "a_r_k", "a_ln_w", "a_ln_b", "final_norm")):
            a = I[name]
            if name == "a_r_k":
                a = a[0].rearrange("(k h) c -> k (h c)", h=2)
            elif name == "final_norm":
                a = a.rearrange("(k c) -> k c", c=P)
            else:
                a = a[0].rearrange("(k c) -> k c", c=P)
            rows.append((1, (16 * n, 16 * n + 16), a))
        for layer in range(2):
            rows.append((2 + layer, 96, I["ada_b"][layer].rearrange("(k c) -> k c", c=P)))
        rows.append((4, (0, 4), I["b_kv_norm"][0].rearrange("(k c) -> k c", c=P)))
        rows.append((4, (4, 5), I["b_kidx_norm"]))
        tables = [(0, 96, PV_MU), (1, 128, PV_W0), (2, 96, PV_ADA), (3, 96, PV_ADA + 96), (4, 5, PV_KVN)]

        self.norms += 1
        with nc.Block() as block:
            @block.sync
            def _(sp):
                sp.dma_start(self.sc[:], I["c"].rearrange("b (p k) -> p (b k)", k=KT)).then_inc(s("c_loaded"), 16)
                for t, r, a in rows:
                    r0, r1 = (0, r) if isinstance(r, int) else r
                    sp.dma_start(self.prow[r0:r1, t, :], a).then_inc(s("rows_loaded"), 16)
                sp.dma_start(self.xin[:], I["x"][0].rearrange("(a p) d -> p a d", p=P)).then_inc(s("x_loaded"), 16)
                for a in range(32):
                    if a >= 6:
                        sp.wait_ge(s("ada_added"), a - 5)
                    sp.dma_start(self.first_ring[a % 6], self.ada_rows(a)).then_inc(s(f"first_loaded{a % 6}"), 16)
                self.load_first(sp, first)

            @block.gpsimd
            def _(pool):
                self.arm(pool, LINEAR_ARMED)
                for t, v in ((self.ident, 0.0), (self.ones, 1.0), (self.blk, 0.0)):
                    nc.gpsimd.memset(t[:], v).then_inc(s("set"), 1)
                for n, v in enumerate((RMS_EPS, GN_EPS, 8 * 0.6931471805599453, 0.0)):
                    nc.gpsimd.memset(self.cst[:, n:n + 1], v).then_inc(s("set"), 1)
                pool.wait_ge(s("set"), 7)
                nc.gpsimd.affine_select(out=self.ident[:], in_=self.ident[:], compare_op=ALU.not_equal, fill=1.0, base=0,
                                        pattern=[[-1, P]], channel_multiplier=1).then_inc(s("ident"), 1)
                pool.wait_ge(s("ident"), 1)
                for h in range(2):
                    nc.gpsimd.memset(self.blk[h * HD:(h + 1) * HD, h * HD:(h + 1) * HD], 1.0).then_inc(s("blk"), 1)
                    pool.wait_ge(s("blk"), h + 1)
                steps = [0]

                def select(out, in_, op, base, pattern, cm):
                    nc.gpsimd.affine_select(out=out, in_=in_, compare_op=op, fill=0.0, base=base, pattern=pattern,
                                            channel_multiplier=cm).then_inc(s("mask_step"), 1)
                    steps[0] += 1
                    pool.wait_ge(s("mask_step"), steps[0])

                def within(t, n):
                    v = t[:].rearrange("p (b q) -> p b q", q=n)
                    select(v, v, ALU.is_ge, 0, [[-n, P // n], [0, n]], 1)
                    select(v, v, ALU.is_ge, n - 1, [[n, P // n], [0, n]], -1)

                select(self.m_B[:], self.blk[:], ALU.is_gt, 0, [[1, P]], -1)
                select(self.m_F[:], self.blk[:], ALU.is_ge, 0, [[1, P]], -1)
                nc.gpsimd.tensor_scalar(self.m_E[:], self.m_F[:], -1.0, None, MUL).then_inc(s("masks"), 1)
                pool.wait_ge(s("masks"), 1)
                select(self.m_A2[:], self.blk[:], ALU.is_gt, 0, [[-1, P]], 1)
                select(self.m_A1[:], self.m_A2[:], ALU.is_gt, 0, [[-1, P]], 1)
                within(self.m_A1, 32)
                nc.gpsimd.tensor_tensor(self.m_A2[:], self.m_A2[:], self.m_A1[:], SUB).then_inc(s("masks"), 1)
                pool.wait_ge(s("masks"), 2)
                select(self.m_D[:], self.m_A1[:], ALU.is_gt, 0, [[-1, P]], 1)
                within(self.m_D, 16)
                nc.gpsimd.tensor_tensor(self.m_A1[:], self.m_A1[:], self.m_D[:], SUB).then_inc(s("masks"), 1)
                pool.wait_ge(s("masks"), 3)
                select(self.m_Xd[:], self.m_B[:], ALU.is_gt, 0, [[1, P]], -1)
                within(self.m_Xd, 16)

            @block.scalar
            def _(act):
                act.wait_ge(s("c_loaded"), 16)
                nc.scalar.activation(self.tmp[:, 0, 0:KT], self.sc[:], ACT.Sigmoid).then_inc(s("sig_c"), 1)
                for n in range(4):
                    act.wait_ge(s("x_turned"), 2 * n + 1)
                    nc.scalar.activation(self.x[:, 4 * n:4 * n + 2, :], ps[:, (2 * n) % 4, :].rearrange("p (m t) -> p m t", m=2),
                                         ACT.Copy).then_inc(s("x_even"), 1)
                act.wait_ge(s("x_even"), 4)
                act.wait_ge(s("x_odd"), 4)
                for n in range(8):
                    if n:
                        act.wait_ge(s("square_added"), n)
                    else:
                        act.wait_ge(s("silu_c"), 1)
                    nc.scalar.activation(self.tmp[:], self.x[:, 2 * n:2 * n + 2, :], ACT.Square).then_inc(s("squared"), 1)
                self.rstd_from_sums(act, 0)

            @block.vector
            def _(dve):
                dve.wait_ge(s("sig_c"), 1)
                nc.vector.tensor_tensor(self.sc[:], self.sc[:], self.tmp[:, 0, 0:KT], MUL).then_inc(s("silu_c"), 1)
                for n in range(4):
                    dve.wait_ge(s("x_turned"), 2 * n + 2)
                    nc.vector.tensor_copy(self.x[:, 4 * n + 2:4 * n + 4, :],
                                          ps[:, (2 * n + 1) % 4, :].rearrange("p (m t) -> p m t", m=2)).then_inc(s("x_odd"), 1)
                dve.wait_ge(s("rows_turned"), 1)
                for n, (t, r, at) in enumerate(tables):
                    nc.vector.tensor_copy(self.pv[:, at:at + r], ps[:, 4 + n // 4, (n % 4) * P:(n % 4) * P + r]).then_inc(s("pv"), 1)
                dve.wait_ge(s("pv"), 5)
                nc.vector.tensor_scalar(self.omu[:], self.pv[:, PV_MU:PV_MU + 96], -1.0, 1.0, MUL, ADD)
                nc.vector.tensor_scalar(self.omka[:], self.pv[:, PV_KA:PV_KA + 16], -1.0, 1.0, MUL, ADD)
                for n in range(8):
                    dve.wait_ge(s("squared"), n + 1)
                    if n == 0:
                        nc.vector.tensor_copy(self.sqfirst[:], self.tmp[:]).then_inc(s("square_added"), 1)
                    else:
                        dve.wait_ge(s("square_added"), n)
                        nc.vector.tensor_tensor(self.sqfirst[:], self.sqfirst[:], self.tmp[:], ADD).then_inc(s("square_added"), 1)
                for piece in range(1, 12, 3):
                    at = slice(PV_ADA + 16 * piece, PV_ADA + 16 * piece + 16)
                    nc.vector.tensor_scalar(self.pv[:, at], self.pv[:, at], 1.0, None, ADD).then_inc(s("one_more"), 1)
                dve.wait_ge(s("one_more"), 4)
                dve.wait_ge(s("silu_c"), 1)
                for piece in range(2):
                    for k in range(KT):
                        a = 16 * piece + k
                        dve.wait_ge(s(f"first_loaded{a % 6}"), 16 * (a // 6 + 1))
                        if k == 0:
                            if piece:
                                dve.wait_ge(s("ada_summed"), piece)
                            nc.vector.tensor_scalar(self.ada_acc[:], self.first_ring[a % 6], self.sc[:, 0:1], None, MUL).then_inc(s("ada_added"), 1)
                        else:
                            dve.wait_ge(s("ada_added"), a)
                            nc.vector.scalar_tensor_tensor(self.ada_acc[:], self.first_ring[a % 6], self.sc[:, k:k + 1],
                                                           self.ada_acc[:], MUL, ADD).then_inc(s("ada_added"), 1)
                        if a == 4:
                            nc.vector.memset(self.hpad[:, :, 0:1], 0.0)
                            dve.wait_ge(s("rstd"), 1)
                            for m in range(KT):
                                nc.vector.tensor_tensor(self.hpad[:, m, 1:T + 1], self.x[:, m, :], self.rstd[:], MUL)
                    self.ada_finish(dve, piece)

            @block.tensor
            def _(pe):
                pe.wait_ge(s("ident"), 1)
                pe.wait_ge(s("rows_loaded"), 16 * len(rows))
                for n, (t, r, at) in enumerate(tables):
                    last = nc.tensor.transpose(ps[:, 4 + n // 4, (n % 4) * P:(n % 4) * P + r], self.prow[0:r, t, :],
                                               self.ident[0:r, 0:r])
                last.then_inc(s("rows_turned"), 1)
                pe.wait_ge(s("x_loaded"), 16)
                for n in range(8):
                    if n >= 4:
                        pe.wait_ge(s("x_even") if n % 2 == 0 else s("x_odd"), n // 2 - 1)
                    for mm in range(2):
                        for a in range(2):
                            last = nc.tensor.transpose(ps[:, n % 4, (2 * mm + a) * P:(2 * mm + a + 1) * P],
                                                       self.xin[:, a, (2 * n + mm) * P:(2 * n + mm + 1) * P], self.ident[:])
                    last.then_inc(s("x_turned"), 1)
                pe.wait_ge(s("square_added"), 8)
                for b in range(2):
                    last = nc.tensor.matmul(ps[:, 6, 0:T], self.ones[:], self.sqfirst[:, b, :], start=b == 0, stop=b == 1)
                last.then_inc(s("sum_square"), 1)
                for piece in range(2):
                    self.ada_sum(pe, piece, piece)

    def sum_squares(self, pe, n0):
        pe.wait_ge(self.s("square_added"), self.squares_at[n0])
        for b in range(2):
            last = self.nc.tensor.matmul(self.ps[:, 6, 0:T], self.ones[:], self.sqacc[:, b, :], start=b == 0, stop=b == 1)
        last.then_inc(self.s("sum_square"), 1)

    def rstd_from_sums(self, act, n0):
        nc, s = self.nc, self.s
        act.wait_ge(s("sum_square"), n0 + 1)
        nc.scalar.activation(self.rstd[:], self.ps[:, 6, 0:T], ACT.Ln, scale=1.0 / D, bias=self.cst[:, 0:1]).then_inc(s("ln_ms"), 1)
        act.wait_ge(s("ln_ms"), n0 + 1)
        nc.scalar.activation(self.rstd[:], self.rstd[:], ACT.Exp, scale=-0.5).then_inc(s("rstd"), 1)

    def modulate_first(self):
        nc = self.nc
        scale = lambda k: self.mod[:, 16 + k:17 + k]
        shift = lambda k: self.mod[:, k:k + 1]
        with nc.Block(no_gpsimd_drain=True) as block:
            @block.scalar
            def _(act):
                for k in range(0, KT, 2):
                    nc.scalar.activation(self.hpad[:, k, 1:T + 1], self.hpad[:, k, 1:T + 1], ACT.Identity, scale=scale(k), bias=shift(k))

            @block.vector
            def _(dve):
                for k in range(1, KT, 2):
                    nc.vector.tensor_scalar(self.hpad[:, k, 1:T + 1], self.hpad[:, k, 1:T + 1], scale(k), shift(k), MUL, ADD)

    def linear(self, name, phase, n, following, act_src, prepare=None, evac=None, ada=(), kt=UK,
               first_loaded=RAW, beside=()):
        nc, s = self.nc, self.s
        s0, p0, c0 = self.split_units, self.pairs, self.cgs
        self.split_units += 8 * n
        self.pairs += n
        self.cgs += n
        a_hi, a_lo = act_src
        size = kt * COLS
        runs, at = [], 0
        for lo, hi, a, per in ada:
            assert a % 2 == 0 and a // 16 == (a + per * (hi - lo) - 1) // 16
            if lo > at:
                runs.append((at, lo, None, 0))
            runs.append((lo, hi, a, per))
            at = hi
        if at < n:
            runs.append((at, n, None, 0))
        sums0 = self.ada_sums
        split_before, self.split_ahead = self.split_ahead, bool(following and "size" in following)
        ahead = following["size"] if self.split_ahead else None

        def over(eng, lo, hi, body):
            if hi - lo == 1:
                body(lo)
            elif hi > lo:
                with eng.Fori(lo, hi) as i:
                    body(i)

        with nc.Block(no_gpsimd_drain=not evac.has_pool) as block:
            @block.sync
            def _(sp):
                for u in range(first_loaded, RAW):
                    self.load_unit(sp, u, phase["source"](0, u))

                def raw_pair(i, source, a, per, r):
                    for u in range(RAW):
                        if source is not None:
                            sp.wait_ge(s("unit_split"), i * 8 + (s0 + u + 1))
                            self.load_unit(sp, u, source(i, u))
                        if a is not None and u % (8 // per) == 1:
                            self.ada_stream(sp, a, per, r, u // (8 // per))
                for lo, hi, a, per in runs:
                    over(sp, lo, min(hi, n - 1), lambda i: raw_pair(i, lambda i, u: phase["source"](i + 1, u), a, per, i - lo))
                raw_pair(n - 1, (lambda i, u: following["source"](0, u)) if following else None, runs[-1][2], runs[-1][3], n - 1 - runs[-1][0])

            @block.scalar
            def _(act):
                for u in range(4):
                    if prepare and u:
                        for k in range(4 * u - 2, 4 * u):
                            prepare.high(act, k)
                    if u == 3 or not split_before:
                        self.split_hi(act, 0, u, s0, p0, size)
                    if prepare:
                        if u == 0:
                            prepare.act_head(act)
                        for k in range(4 * u, 4 * u + 2):
                            prepare.high(act, k)
                if prepare:
                    for k in range(KT - 2, KT):
                        prepare.high(act, k)

                def half(i):
                    for u in range(4, 8):
                        self.split_hi(act, i, u, s0, p0, size)
                    evac.act(act, i, 0, s0 + 4)
                    for m in beside:
                        m.beside_act(act, i, 0)

                def body(i):
                    half(i)
                    for u in range(4):
                        self.split_hi(act, i + 1, u, s0, p0, size)
                    evac.act(act, i, 1, s0 + 8)
                    for m in beside:
                        m.beside_act(act, i, 1)
                if s0 == 0:
                    body(0)
                over(act, 0 if s0 else 1, n - 1, body)
                half(n - 1)
                if ahead:
                    for u in range(3):
                        self.split_hi(act, n, u, s0, p0, ahead)
                evac.act(act, n - 1, 1, s0 + 8)
                for m in beside:
                    m.beside_act(act, n - 1, 1)

            @block.vector
            def _(dve):
                evac.dve_start(dve)
                for u in range(4):
                    if u == 3 or not split_before:
                        self.split_lo(dve, 0, u, s0, size)
                    if prepare:
                        if u == 0:
                            prepare.dve_head(dve)
                        else:
                            for k in range(4 * u - 2, 4 * u):
                                prepare.low(dve, k)
                        for k in range(4 * u, 4 * u + 4):
                            prepare.first(dve, k)
                            if k >= 4 * u + 2:
                                prepare.low(dve, k - 2)
                if prepare:
                    for k in range(KT - 2, KT):
                        prepare.low(dve, k)
                for lo, hi, a, per in runs:
                    if a is not None and a % 16 == 0:
                        self.ada_zero(dve)

                    def body(i, tail=False):
                        def adas(u):
                            if a is not None and (u + 1) % (8 // per) == 0:
                                self.ada_add(dve, a, per, i - lo, (u + 1) // (8 // per) - 1)
                        for u in range(4, 8):
                            adas(u - 4)
                            self.split_lo(dve, i, u, s0, size)
                        evac.dve(dve, i, 0, s0 + 4)
                        for m in beside:
                            m.beside_dve(dve, i, 0)
                        for u in range(4):
                            adas(u + 4)
                            if not tail:
                                self.split_lo(dve, i + 1, u, s0, size)
                            elif ahead and u < 3:
                                self.split_lo(dve, n, u, s0, ahead)
                        evac.dve(dve, i, 1, s0 + 8)
                        for m in beside:
                            m.beside_dve(dve, i, 1)
                    over(dve, lo, min(hi, n - 1), body)
                    if hi == n:
                        body(n - 1, True)
                    if a is not None and (a + per * (hi - lo)) % 16 == 0:
                        self.ada_finish(dve, a // 16)

            @block.tensor
            def _(pe):
                if prepare:
                    prepare.pe_head(pe)
                sums = sums0
                for lo, hi, a, per in runs:
                    def body(i):
                        for g in range(2):
                            pe.wait_ge(s(f"group_taken{g}"), i + (c0 + 1))
                            for q in range(4):
                                u = 4 * g + q
                                pe.wait_ge(s("unit_split"), i * 8 + (s0 + u + 1))
                                if prepare and g == 0:
                                    pe.wait_ge(s("act_ready"), prepare.a0 + kt * (q + 1))
                                self.multiply(u, kt, kt * q, 4 * kt, COLS, ((0, P), (P, 2 * P)), a_hi, a_lo,
                                              (2 * g, 2 * g + 1)).then_inc(s("unit_used"), 1)
                    over(pe, lo, hi, body)
                    if a is not None and (a + per * (hi - lo)) % 16 == 0:
                        self.ada_sum(pe, a // 16, sums)
                        sums += 1

            if evac.has_pool:
                @block.gpsimd
                def _(pool):
                    evac.pool(pool)

    def loras(self, following):
        nc, s, ps, I = self.nc, self.s, self.ps, self.i
        p0, n0, m0, c0 = self.pairs, self.natives, self.mixes, self.cgs
        self.pairs += 2
        self.natives += 16
        self.cgs_stored = c0 + 12
        w2, a2, g2 = I["a_w2"][0], I["a_a2"][0], I["a_g2"][0].rearrange("(k p) n -> p k n", p=P)

        def outer(i, u):
            if u < 4:
                return (w2 if u < 2 else a2)[:, (u % 2) * 1024:(u % 2 + 1) * 1024], (1024,)
            return g2[:, :, (u - 4) * 512:(u - 3) * 512], (2, 512)
        groups = [(q, n) for q in range(3) for n in range(8)]

        mixed = MixedWhole(self, [(4, self.lmix[1])])
        with nc.Block() as block:
            @block.sync
            def _(sp):
                for u in range(RAW):
                    sp.wait_ge(s("native_used"), n0 + u + 1)
                    self.load_unit(sp, u, outer(0, u))
                for u in range(EARLY):
                    sp.wait_ge(s("native_used"), n0 + 8 + u + 1)
                    self.load_unit(sp, u, following["source"](0, u))

            @block.scalar
            def _(act):
                for k in range(KT):
                    mixed.act_one(act, 4, k, k, k)
                act.wait_ge(s("lora_w"), 1)
                nc.scalar.activation(self.lhid[0:96, 0, :], ps[0:96, 4, 0:T], ACT.Tanh).then_inc(s("lora_hid"), 1)
                act.wait_ge(s("lora_a"), 1)
                nc.scalar.activation(self.lhid[0:96, 1, :], ps[0:96, 5, 0:T], ACT.Copy).then_inc(s("lora_hid"), 1)
                act.wait_ge(s("lora_g"), 1)
                nc.scalar.activation(self.lhid[:, 2:4, :], ps[:, 6:8, 0:T], ACT.Sigmoid).then_inc(s("lora_hid"), 1)
                for n, (q, t) in enumerate(groups):
                    act.wait_ge(s("lora_out"), n + 1)
                    act.wait_ge(s(f"stored{n % 2}"), 16 * (c0 + n // 2))
                    o = ps[:, n % 4, :].rearrange("p (m t) -> p m t", m=2)
                    if q == 2:
                        last = nc.scalar.activation(self.stg[:, n % 2], o, ACT.Copy)
                    else:
                        for b in range(2):
                            at = (PV_W0, PV_A0)[q] + 2 * t + b
                            last = nc.scalar.activation(self.stg[:, n % 2, b], o[:, b], ACT.Sigmoid, bias=self.pv[:, at:at + 1])
                    last.then_inc(s("lora_taken"), 1)

            @block.vector
            def _(dve):
                for k in range(KT):
                    mixed.dve_one(dve, 4, self.lmix[1], k, k, k)

            @block.gpsimd
            def _(pool):
                self.arm(pool, RWKV_ARMED)
                for n, (q, t) in enumerate(groups):
                    pool.wait_ge(s("lora_taken"), n + 1)
                    pool.dma_start(self.scr[3 + q, 2 * t:2 * t + 2].rearrange("m p t -> p m t"), self.stg[:, n % 2]).then_inc(s(f"stored{n % 2}"), 16)

            @block.tensor
            def _(pe):
                for n, (units, kt, cols, banks, done) in ((0, ((0, 1), 8, 96, (4,), "lora_w")), (2, ((2, 3, 4, 5), 4, 256, (6, 7), "lora_g")),
                                                         (1, ((6, 7), 8, 96, (5,), "lora_a"))):
                    for u in units:
                        pe.wait_ge(s(f"unit_loaded{u}"), 16 * (p0 + 1))
                        w = self.raw[:, u, 0:kt * cols].rearrange("p (k n) -> p k n", k=kt)
                        k0 = (u - units[0]) * kt
                        if n == 1:
                            pe.wait_ge(s("mixed"), m0 + k0 + kt)
                        for b, bank in enumerate(banks):
                            width = min(cols, P)
                            for kk in range(kt):
                                last = nc.tensor.matmul(ps[0:width, bank, 0:T], w[:, kk, b * P:b * P + width], self.lmix[n][:, k0 + kk, :],
                                                        start=k0 + kk == 0, stop=k0 + kk == KT - 1)
                        last.then_inc(s("native_used"), 1)
                    pe.wait_ge(s("native_used"), n0 + units[-1] + 1)
                    nc.tensor.nop().then_inc(s(done), 1)
                for n, (q, t) in enumerate(groups):
                    if t == 0:
                        pe.wait_ge(s("lora_hid"), q + 1)
                    per = 4 if q < 2 else 2
                    u = 2 * q + t // per if q < 2 else 4 + t // per
                    if t % per == 0:
                        pe.wait_ge(s(f"unit_loaded{u}"), 16 * (p0 + 2))
                    if n >= 4:
                        pe.wait_ge(s("lora_taken"), n - 3)
                    for b in range(2):
                        m = (t % per) * 2 + b
                        o = ps[:, n % 4, b * T:(b + 1) * T]
                        if q < 2:
                            last = nc.tensor.matmul(o, self.raw[0:96, u, m * P:(m + 1) * P], self.lhid[0:96, q, :], start=True, stop=True)
                        else:
                            for kk in range(2):
                                last = nc.tensor.matmul(o, self.raw[:, u, kk * 512 + m * P:kk * 512 + (m + 1) * P],
                                                        self.lhid[:, 2 + kk, :], start=kk == 0, stop=kk == 1)
                    if t % per == per - 1:
                        last.then_inc(s("native_used"), 1)
                        pe.wait_ge(s("native_used"), n0 + 8 + u + 1)
                        nc.tensor.nop().then_inc(s("lora_out"), 1)
                    else:
                        last.then_inc(s("lora_out"), 1)

    def rwkv(self):
        nc, s, ps, R = self.nc, self.s, self.ps, self.R
        H = (slice(0, HD), slice(HD, P))

        def bc(mask):
            return mask[:].unsqueeze(1).to_broadcast([P, NC, P])

        def bank4(j, b):
            return ps[:, 4 * j + b, :].rearrange("p (c n) -> p c n", c=NC)

        sums0 = self.ada_sums
        self.ada_sums += KT // 2

        L = KT // 2


        def wait(eng, name, v):
            if not (isinstance(v, int) and v <= 0):
                eng.wait_ge(s(name), v)

        def at(eng, i, name, j):
            wait(eng, name, i * 2 + (j + 1 + one(name)))

        def past(eng, i, name):
            wait(eng, name, i * 2 + one(name))

        def past2(eng, i, name):
            wait(eng, name, i * 2 + (one(name) - 2))

        def ada_half(dve, i, n):
            u, h = divmod(n, 2)
            dve.wait_ge(s(f"ada_loaded{u % 2}"), i * 64 + 16 * (u // 2 + 1))
            if u == 0:
                wait(dve, "ada_summed", i + sums0)
            else:
                dve.wait_ge(s("ada_added"), i * 8 + (32 + u))
            acc, row = self.ada_acc[:, h * 1024:(h + 1) * 1024], self.ada_ring[:, u % 2, h * 1024:(h + 1) * 1024]
            if u == 0:
                last = nc.vector.tensor_scalar(acc, row, self.sc[:, n:n + 1], None, MUL)
            else:
                last = nc.vector.scalar_tensor_tensor(acc, row, self.sc[:, n:n + 1], acc, MUL, ADD)
            if h:
                last.then_inc(s("ada_added"), 1)

        def wide(j, b, part):
            return ps[:, 4 * j + b:4 * j + b + 2, :].rearrange("p b (c q n) -> p (b c) q n", c=2, q=2)[:, :, part, :]

        with nc.Block() as block:
            @block.sync
            def _(sp):
                view = self.i["ada_w"][0].rearrange("(p k) n -> p k n", k=KT)

                def ada(i, u):
                    sp.wait_ge(s("ada_added"), i * 8 + (32 + u - 1))
                    self.ada_load(sp, view[:, 2 * u:2 * u + 2, bass.ds(i * 1024 + 2 * D, 1024)], u % 2)

                def tiles(i):
                    for j in range(2):
                        for n in ("bon", "vb", "rho"):
                            past(sp, i, n)
                        sp.dma_start(R[j]["in"][:], self.scr[0:5, bass.ds(i * 2 + j, 1)].rearrange("q m p t -> p (q m) t")).then_inc(s(f"in_loaded{j}"), 16)

                def gates(i):
                    for j in range(2):
                        past(sp, i, "yg")
                        sp.dma_start(R[j]["g"][:], self.scr[5, bass.ds(i * 2 + j, 1)].rearrange("m p t -> p (m t)")).then_inc(s(f"g_loaded{j}"), 16)

                def body(i, more):
                    for u in (6, 7):
                        ada(i, u)
                    for u in range(4):
                        ada(i + 1, u)
                    if more:
                        tiles(i + 2)
                    for u in (4, 5):
                        ada(i + 1, u)
                    gates(i + 1)
                for g in range(2):
                    sp.wait_ge(s(f"stored{g}"), 16 * self.cgs_stored)
                tiles(0)
                for u in range(4):
                    ada(0, u)
                tiles(1)
                for u in (4, 5):
                    ada(0, u)
                gates(0)
                with sp.Fori(0, L - 2) as i:
                    body(i, True)
                body(L - 2, False)
                for u in (6, 7):
                    ada(L - 1, u)

            @block.scalar
            def _(act):
                def copy(name, dst, src, scale=1.0):
                    nc.scalar.activation(dst, src, ACT.Copy, scale=scale).then_inc(s(name), 1)

                def prep_v(i):
                    for j in range(2):
                        b = R[j]
                        act.wait_ge(s(f"in_loaded{j}"), i * 16 + 16)
                        act.wait_ge(s("bd_zeroed"), 8)
                        past(act, i, "tok_V")
                        for h in range(2):
                            last = nc.scalar.activation(b["vb"][H[h], :, H[h]], chunks(b["in"][H[h], 2, :]), ACT.Copy)
                        last.then_inc(s("vb"), 1)
                        at(act, i, "q1", j)
                        nc.scalar.activation(b["kk"][:], b["q1"][:], ACT.Square).then_inc(s("sq"), 1)

                def prep_exp(i):
                    for j in range(2):
                        b = R[j]
                        at(act, i, "Ls", j)
                        past(act, i, "Pi_end")
                        nc.scalar.activation(b["Pi"][:], b["Ls"][:], ACT.Exp, scale=DEC).then_inc(s("Pi"), 1)
                        nc.scalar.activation(b["Pn"][:], b["Ls"][:], ACT.Exp, scale=-DEC).then_inc(s("Pn"), 1)
                        at(act, i, "Lx", j)
                        nc.scalar.activation(b["Px"][:], b["Px"][:], ACT.Exp, scale=DEC).then_inc(s("Px"), 1)

                def prep_norm(i):
                    for j in range(2):
                        at(act, i, "ssc", j)
                        nc.scalar.activation(R[j]["rk"][:], R[j]["rk"][:], ACT.Ln, scale=65536.0).then_inc(s("lnk"), 1)
                    for j in range(2):
                        at(act, i, "lnk", j)
                        nc.scalar.activation(R[j]["rk"][:], R[j]["rk"][:], ACT.Exp, scale=-0.5, bias=self.cst[:, 2:3]).then_inc(s("rkn"), 1)

                def stage_M(i, post):
                    for j in range(2) if post else ():
                        at(act, i - 1, "Yp", j)
                        at(act, i, "ka", j)
                        nc.scalar.activation(chunks(R[j]["q1"][H[0], :]), bank4(j, 0)[H[0], :, H[0]], ACT.Copy).then_inc(s("y0"), 1)
                    for j in range(2):
                        at(act, i, "M1", j)
                        copy("Pi_end", R[j]["Pi_end"][:, 0:NC], chunks(R[j]["Pi"][:])[:, :, C - 1])
                        copy("rho_al_now", R[j]["rho_al_now"][:].rearrange("p c q n -> p (c q n)"),
                             R[j]["rho_al"][:].rearrange("p c q n -> p (c q n)"))
                    for j in range(2):
                        at(act, i, "tokp_V", j)
                        copy("tok_V", R[j]["Vt"][:], bank4(j, 1))
                    for j in range(2) if post else ():
                        ycsq(i - 1, j)
                    for j in range(2):
                        at(act, i, "tokp_K", j)
                        copy("tok_K", R[j]["Kt"][:], bank4(j, 2))
                    if post:
                        inverse_root(i - 1)

                def ycsq(i, j):
                    at(act, i, "yc", j)
                    nc.scalar.activation(R[j]["rk"][:], R[j]["kk"][:], ACT.Square).then_inc(s("ycsq"), 1)

                def inverse_root(i):
                    for j in range(2):
                        at(act, i, "varp", j)
                        nc.scalar.activation(R[j]["Px"][:], ps[:, 4 * j + 3, T:2 * T], ACT.Ln, scale=1.0 / HD, bias=self.cst[:, 1:2]).then_inc(s("lnv"), 1)
                    for j in range(2):
                        at(act, i, "lnv", j)
                        nc.scalar.activation(R[j]["Px"][:], R[j]["Px"][:], ACT.Exp, scale=-0.5).then_inc(s("rsv"), 1)

                def stage_N(i, prep):
                    for name, bank, dst in (("D2", 0, "D2"), ("X2", 1, "X2"), ("tok_B", 3, "Bt"), ("D4", 2, "Dd"), ("X4", 3, "Xd"),
                                            ("D8", 1, "D2"), ("T16", 3, "X2"), ("T32", 3, "X2")):
                        for j in range(2):
                            at(act, i, "tokp_B" if name == "tok_B" else name + "p", j)
                            copy(name, R[j][dst][:], bank4(j, bank), -1.0 if name == "tok_B" else 1.0)
                        if name == "X4":
                            for j in range(2):
                                past(act, i, "yb")
                                at(act, i, "bon", j)
                                copy("bon_now", R[j]["bon_now"][:], R[j]["bon"][:])
                        if prep and name == "X4":
                            prep_v(i + 1)
                        if prep and name == "D8":
                            prep_exp(i + 1)
                    if prep:
                        prep_norm(i + 1)

                def stage_C(i):
                    for c in range(NC):
                        for j in range(2):
                            act.wait_ge(s("Rp"), i * 8 + (2 * c + j + 1))
                            copy("R", R[j]["Rr"][:], ps[:, 4 * j + 2, c * P:(c + 1) * P])
                        if c < NC - 1:
                            for j in range(2):
                                act.wait_ge(s("Sp"), i * 6 + (2 * c + j + 1))
                                nc.scalar.activation(R[j]["S"][:], ps[:, 4 * j + 1, c * P:(c + 1) * P], ACT.Copy,
                                                     scale=R[j]["Pi_end"][:, c:c + 1]).then_inc(s("S"), 1)
                prep_v(0)
                prep_exp(0)
                prep_norm(0)
                stage_M(0, False)
                with act.Fori(0, L - 1) as i:
                    stage_N(i, True)
                    stage_C(i)
                    stage_M(i + 1, True)
                stage_N(L - 1, False)
                stage_C(L - 1)
                for j in range(2):
                    at(act, L - 1, "Yp", j)
                    nc.scalar.activation(chunks(R[j]["q1"][H[0], :]), bank4(j, 0)[H[0], :, H[0]], ACT.Copy).then_inc(s("y0"), 1)
                for j in range(2):
                    ycsq(L - 1, j)
                inverse_root(L - 1)

            @block.vector
            def _(dve):
                def tt(name, out, a, b, op):
                    nc.vector.tensor_tensor(out, a, b, op).then_inc(s(name), 1)

                def col(i, first, j):
                    return self.pv[:, bass.ds(i * 2 + (first + j), 1)]

                def prep_a(i):
                    for j in range(2):
                        b = R[j]
                        dve.wait_ge(s(f"in_loaded{j}"), i * 16 + 16)
                        past2(dve, i, "yg")
                        nc.vector.tensor_scalar(b["q1"][:], b["in"][:, 1, :], col(i, PV_KK, j), None, MUL).then_inc(s("q1"), 1)
                        past(dve, i, "Pn")
                        for c in range(NC):
                            t = slice(c * C, (c + 1) * C)
                            last = nc.vector.tensor_tensor_scan(b["Ls"][:, t], self.ones[:, 0:C], b["in"][:, 3, t], 0.0, MUL, ADD)
                        last.then_inc(s("Ls"), 1)

                def prep_b(i, j):
                    b = R[j]
                    r, k, v, sw, a = (b["in"][:, q, :] for q in range(5))
                    past2(dve, i, "yn")
                    at(dve, i, "Ls", j)
                    tt("Lx", b["Px"][:], b["Ls"][:], sw, SUB)
                    past2(dve, i, "y_lo")
                    nc.vector.tensor_scalar(b["k2"][:], a, col(i, PV_KA, j), self.omka[:, bass.ds(i * 2 + j, 1)], MUL, ADD).then_inc(s("t1"), 1)
                    at(dve, i, "t1", j)
                    tt("k2", b["k2"][:], b["k2"][:], k, MUL)
                    at(dve, i, "k2", j)
                    past(dve, i, "bon_now")
                    nc.vector.scalar_tensor_tensor(b["bon"][:], r, col(i, PV_RK, j), b["k2"][:], MUL, MUL).then_inc(s("rb"), 1)

                def prep_c(i):
                    for j in range(2):
                        b = R[j]
                        at(dve, i, "rbs", j)
                        past2(dve, i, "lnv")
                        nc.vector.tensor_scalar(b["rk"][:], ps[:, 4 * j + 2, 0:T], 1e-24, None, MAX).then_inc(s("ssc"), 1)
                        tt("bon", b["bon"][:], ps[:, 4 * j + 2, T:2 * T], b["in"][:, 2, :], MUL)

                def prep_d(i, j):
                    b = R[j]
                    at(dve, i, "rkn", j)
                    tt("kkn", b["kk"][:], b["q1"][:], b["rk"][:], MUL)
                    at(dve, i, "kkn", j)
                    tt("kka", b["q1"][:], b["kk"][:], b["in"][:, 4, :], MUL)
                    past(dve, i, "rho_al_now")
                    past(dve, i, "tokp_B")
                    at(dve, i, "Px", j)
                    for name, dst, x_, y_ in (("al", b["rho_al"][:, :, 0], b["kk"], b["Px"]), ("rho", b["rho_al"][:, :, 1], None, b["Pi"])):
                        product(name, dst, b["in"][:, 0, :] if x_ is None else x_, y_)

                def prep_e(i, j):
                    b = R[j]
                    at(dve, i, "kka", j)
                    product("be", b["be"], b["q1"], b["Pn"])
                    product("ka", b["ka"], b["k2"], b["Pn"])

                def product(name, dst, x_, y_):
                    for h in range(2):
                        last = nc.vector.tensor_tensor(dst[H[h], :, H[h]], chunks(x_[H[h], :]), chunks(y_[H[h], :]), MUL)
                    last.then_inc(s(name), 1)

                def stage_M(i, post):
                    for j in range(2):
                        b = R[j]
                        past(dve, i, "Yp")
                        at(dve, i, "ka", j)
                        if post:
                            nc.vector.tensor_copy(chunks(b["q1"][H[1], :]), bank4(j, 0)[H[1], :, H[1]]).then_inc(s("y1"), 1)
                        nc.vector.memset(b["S"][:], 0.0).then_inc(s("S0"), 1)
                    for j in range(2):
                        b = R[j]
                        at(dve, i, "M2", j)
                        tt("B", b["B"][:], wide(j, 2, 0), bc(self.m_B), MUL)
                        tt("F", b["F"][:], wide(j, 2, 1), bc(self.m_F), MUL)
                    for j in range(2):
                        b = R[j]
                        at(dve, i, "M1", j)
                        tt("Xd", b["Xd"][:], wide(j, 0, 0), bc(self.m_Xd), MUL)
                        tt("E", b["E"][:], wide(j, 0, 1), bc(self.m_E), MUL)
                    for j in range(2):
                        b = R[j]
                        if post:
                            centred(i - 1, j)
                        at(dve, i, "Xd", j)
                        tt("P1", b["W"][:], bc(self.ident), b["Xd"][:], SUB)
                    for j in range(2):
                        b = R[j]
                        at(dve, i, "M3", j)
                        tt("Dd", b["Dd"][:], bank4(j, 0), bc(self.m_D), MUL)
                        tt("A1", b["A1"][:], bank4(j, 0), bc(self.m_A1), MUL)
                        tt("A2", b["A2"][:], bank4(j, 0), bc(self.m_A2), MUL)

                def centred(i, j):
                    at(dve, i, "meanp", j)
                    nc.vector.scalar_tensor_tensor(R[j]["kk"][:], ps[:, 4 * j + 3, 0:T], -1.0 / HD, R[j]["q1"][:], MUL, ADD).then_inc(s("yc"), 1)

                def gated(i):
                    for j in range(2):
                        b = R[j]
                        at(dve, i, "rsv", j)
                        tt("yn", b["q1"][:], b["kk"][:], b["Px"][:], MUL)
                    for j in range(2):
                        b = R[j]
                        at(dve, i, "yn", j)
                        nc.vector.tensor_scalar(b["q1"][:], b["q1"][:], col(i, PV_LNW, j), col(i, PV_LNB, j), MUL, ADD).then_inc(s("yln"), 1)
                    for j in range(2):
                        b = R[j]
                        at(dve, i, "yln", j)
                        at(dve, i, "bon_now", j)
                        tt("yb", b["q1"][:], b["q1"][:], b["bon_now"][:], ADD)
                    for j in range(2):
                        b = R[j]
                        at(dve, i, "yb", j)
                        dve.wait_ge(s(f"g_loaded{j}"), i * 16 + 16)
                        tt("yg", b["k2"][:], b["q1"][:], b["g"][:], MUL)
                    for j in range(2):
                        at(dve, i, "yg", j)
                        nc.vector.tensor_copy(self.hid_hi[:, bass.ds(i * 2 + j, 1), :], R[j]["k2"][:].unsqueeze(1)).then_inc(s("y_hi"), 1)
                    for j in range(2):
                        at(dve, i, "y_hi", j)
                        m = bass.ds(i * 2 + j, 1)
                        tt("y_lo", self.hid_lo[:, m, :], R[j]["k2"][:].unsqueeze(1), self.hid_hi[:, m, :].bitcast(F32), SUB)

                def stage_N(i, prep):
                    if prep:
                        prep_a(i + 1)
                    ada_half(dve, i, 9)
                    for name, bank, op, prev in (("P2", 0, ADD, "P1"), ("P3", 0, ADD, "P2"), ("P4", 2, ADD, "P3"), ("Z1", 1, None, None),
                                                 ("W32", 0, SUB, "P4"), ("Z2", 1, None, None), ("W64", 0, SUB, "W32")):
                        for j in range(2):
                            b = R[j]
                            at(dve, i, name + "p", j)
                            if op is None:
                                nc.vector.tensor_copy(b["Xd"][:], bank4(j, bank)).then_inc(s(name), 1)
                            else:
                                at(dve, i, prev, j)
                                tt(name, b["W"][:], b["W"][:], bank4(j, bank), op)
                        if prep and name in ("P2", "P3"):
                            prep_b(i + 1, 0 if name == "P2" else 1)
                        if prep and name == "W32":
                            prep_c(i + 1)
                        for n in {"P3": (10,), "P4": (11, 12), "Z1": (13, 14), "W32": (15,)}.get(name, ()):
                            ada_half(dve, i, n)
                    dve.wait_ge(s("ada_summed"), i + (sums0 + 1))
                    nc.vector.tensor_tensor(self.mod[:, bass.ds(i * 8 + 32, 8)], ps[:, 1, 0:8],
                                            self.pv[:, bass.ds(i * 8 + (PV_ADA + 32), 8)], ADD).then_inc(s("mod_ready"), 1)

                def stage_C(i, prep):
                    for c in range(NC):
                        for j in range(2):
                            dve.wait_ge(s("Up"), i * 8 + (2 * c + j + 1))
                            nc.vector.tensor_copy(R[j]["Uu"][:], ps[:, 4 * j + 3, c * P:(c + 1) * P]).then_inc(s("U"), 1)
                        if prep and c < 2:
                            prep_d(i + 1, c)
                            prep_e(i + 1, c)
                        if prep:
                            for n in ((), (), (0, 1, 2), (3, 4))[c]:
                                ada_half(dve, i + 1, n)

                for j in range(2):
                    for n in ("rho_al", "be", "ka", "vb"):
                        nc.vector.memset(R[j][n][:], 0.0).then_inc(s("bd_zeroed"), 1)
                dve.wait_ge(s("bd_zeroed"), 8)
                prep_a(0)
                for j in range(2):
                    prep_b(0, j)
                prep_c(0)
                for j in range(2):
                    prep_d(0, j)
                    prep_e(0, j)
                stage_M(0, False)
                for n in range(9):
                    ada_half(dve, 0, n)
                with dve.Fori(0, L - 1) as i:
                    stage_N(i, True)
                    stage_C(i, True)
                    stage_M(i + 1, True)
                    for n in range(5, 8):
                        ada_half(dve, i + 1, n)
                    gated(i)
                    ada_half(dve, i + 1, 8)
                stage_N(L - 1, False)
                stage_C(L - 1, False)
                for j in range(2):
                    at(dve, L - 1, "Yp", j)
                    nc.vector.tensor_copy(chunks(R[j]["q1"][H[1], :]), bank4(j, 0)[H[1], :, H[1]]).then_inc(s("y1"), 1)
                for j in range(2):
                    centred(L - 1, j)
                gated(L - 1)

            @block.tensor
            def _(pe):
                def mm4(name, j, bank, lhsT, rhs):
                    for c in range(NC):
                        last = nc.tensor.matmul(ps[:, 4 * j + bank, c * P:(c + 1) * P], lhsT[:, c], rhs[:, c], start=True, stop=True)
                    last.then_inc(s(name), 1)

                def turn4(name, j, bank, src):
                    for c in range(NC):
                        last = nc.tensor.transpose(ps[:, 4 * j + bank, c * P:(c + 1) * P], src[:, c], self.ident[:])
                    last.then_inc(s(name), 1)

                def prep(i):
                    for j in range(2):
                        b = R[j]
                        at(pe, i, "sq", j)
                        nc.tensor.matmul(ps[:, 4 * j + 2, 0:T], self.blk[:], b["kk"][:], start=True, stop=True)
                        at(pe, i, "rb", j)
                        nc.tensor.matmul(ps[:, 4 * j + 2, T:2 * T], self.blk[:], b["bon"][:], start=True, stop=True).then_inc(s("rbs"), 1)

                def products(name, i, j, bank, lhsT):
                    for c in range(NC):
                        last = nc.tensor.matmul(ps[:, 4 * j + bank + c // 2, (c % 2) * 256:(c % 2 + 1) * 256], lhsT[:, c],
                                                R[j]["rho_al"][:, c].rearrange("p q n -> p (q n)"), start=True, stop=True)
                    last.then_inc(s(name), 1)

                def mean(i, j):
                    nc.tensor.matmul(ps[:, 4 * j + 3, 0:T], self.blk[:], R[j]["q1"][:], start=True, stop=True).then_inc(s("meanp"), 1)

                def var(i, j):
                    at(pe, i, "ycsq", j)
                    nc.tensor.matmul(ps[:, 4 * j + 3, T:2 * T], self.blk[:], R[j]["rk"][:], start=True, stop=True).then_inc(s("varp"), 1)

                def stage_M(i, post):
                    for j in range(2):
                        at(pe, i, "ka", j)
                        if not post:
                            at(pe, i, "bon", j)
                        products("M2", i, j, 2, R[j]["ka"])
                    for j in range(2):
                        if post:
                            past(pe, i, "y0")
                            past(pe, i, "y1")
                        products("M1", i, j, 0, R[j]["be"])
                    for j in range(2) if post else ():
                        at(pe, i, "F", j)
                        mean(i - 1, j)
                    for j in range(2):
                        at(pe, i, "E", j)
                        mm4("M3", j, 0, R[j]["rho_al"][:, :, 0], R[j]["be"])
                    for j in range(2):
                        at(pe, i, "vb", j)
                        turn4("tokp_V", j, 1, R[j]["vb"])
                    for j in range(2):
                        at(pe, i, "F", j)
                        turn4("tokp_K", j, 2, R[j]["ka"])
                    for j in range(2) if post else ():
                        var(i - 1, j)

                steps = (
                    ("D2p", 0, "Xd", "Dd", ("A2",)), ("X2p", 1, "Dd", "Xd", ("tok_V",)), ("tokp_B", 3, "be", None, ()),
                    ("D4p", 2, "X2", "D2", ("D2", "X2", "tok_K")), ("X4p", 3, "D2", "X2", ("tok_B",)),
                    ("P2p", 0, "D2", "W", ("P1",)),
                    ("D8p", 1, "Xd", "Dd", ("D4", "X4")), ("P3p", 0, "Dd", "W", ("P2",)),
                    ("P4p", 2, "D2", "W", ("D8", "P3")),
                    ("T16p", 3, "W", None, ("P4",)), ("Z1p", 1, "A1", "W", ()),
                    ("W32p", 0, "X2", "Xd", ("T16", "Z1")),
                    ("T32p", 3, "W", None, ("W32",)), ("Z2p", 1, "A2", "W", ()),
                    ("W64p", 0, "X2", "Xd", ("T32", "Z2")),
                )

                def stage_N(i, more):
                    for name, bank, lhsT, rhs, needs in steps:
                        for j in range(2):
                            if name == "tokp_B":
                                past(pe, i, "lnv")
                            for n in needs:
                                at(pe, i, n, j)
                            if rhs is None:
                                turn4(name, j, bank, R[j][lhsT])
                            else:
                                mm4(name, j, bank, R[j][lhsT], R[j][rhs])
                        if more and name == "W32p":
                            prep(i + 1)
                    pe.wait_ge(s("ada_added"), i * 8 + 40)
                    for m in range(8):
                        for h in range(2):
                            last = nc.tensor.matmul(ps[:, 1, m:m + 1], self.ada_acc[:, (8 * h + m) * P:(8 * h + m + 1) * P],
                                                    self.ones[:, 0:1], start=h == 0, stop=h == 1)
                    last.then_inc(s("ada_summed"), 1)

                def stage_C(i, more):
                    for c in range(NC):
                        col = slice(c * P, (c + 1) * P)
                        for j in range(2):
                            b = R[j]
                            if c == 0:
                                at(pe, i, "S0", j)
                                at(pe, i, "rho_al_now", j)
                                if more:
                                    at(pe, i + 1, "bon", j)
                            else:
                                pe.wait_ge(s("S"), i * 6 + (2 * (c - 1) + j + 1))
                            o = ps[:, 4 * j + 2, col]
                            nc.tensor.matmul(o, b["B"][:, c], b["Vt"][:, c], start=True, stop=False)
                            nc.tensor.matmul(o, b["rho_al_now"][:, c, 0], b["S"][:], start=False, stop=True).then_inc(s("Rp"), 1)
                        for j in range(2):
                            b = R[j]
                            o = ps[:, 4 * j, col]
                            if c == 0:
                                at(pe, i, "W64", j)
                            nc.tensor.matmul(o, b["Vt"][:, c], b["F"][:, c], start=True, stop=False)
                            nc.tensor.matmul(o, b["S"][:], b["rho_al_now"][:, c, 1], start=False, stop=False)
                            pe.wait_ge(s("R"), i * 8 + (2 * c + j + 1))
                            nc.tensor.matmul(ps[:, 4 * j + 3, col], b["W"][:, c], b["Rr"][:], start=True, stop=True).then_inc(s("Up"), 1)
                        for j in range(2):
                            b = R[j]
                            if c < NC - 1:
                                o = ps[:, 4 * j + 1, col]
                                if c == 0 and j == 0:
                                    pe.wait_ge(s("mod_ready"), i + (sums0 + 1))
                                nc.tensor.matmul(o, b["Kt"][:, c], b["Vt"][:, c], start=True, stop=False)
                                nc.tensor.matmul(o, self.ident[:], b["S"][:], start=False, stop=False)
                                pe.wait_ge(s("U"), i * 8 + (2 * c + j + 1))
                                nc.tensor.matmul(o, b["Bt"][:, c], b["Uu"][:], start=False, stop=True).then_inc(s("Sp"), 1)
                            else:
                                pe.wait_ge(s("U"), i * 8 + (2 * c + j + 1))
                            last = nc.tensor.matmul(ps[:, 4 * j, col], b["Uu"][:], b["E"][:, c], start=False, stop=True)
                            if c == NC - 1:
                                last.then_inc(s("Yp"), 1)

                prep(0)
                stage_M(0, False)
                with pe.Fori(0, L - 1) as i:
                    stage_N(i, True)
                    stage_C(i, True)
                    stage_M(i + 1, True)
                stage_N(L - 1, False)
                stage_C(L - 1, False)
                for j in range(2):
                    at(pe, L - 1, "y0", j)
                    at(pe, L - 1, "y1", j)
                    mean(L - 1, j)
                for j in range(2):
                    var(L - 1, j)

    def ffn(self, layer, pieces, following):
        I = self.i
        w1, w3 = (I[n][layer].rearrange("(k p) n -> p k n", p=P) for n in ("f_w1", "f_w3"))
        w2 = I["f_w2"][layer]
        runs = ((0, 16), (16, 16), (32, 12))
        phases = []
        for t0, nt in runs:
            def up(i, u, t0=t0):
                q = u % 4
                return (w1 if u < 4 else w3)[:, q * UK:(q + 1) * UK, bass.ds(i * COLS + t0 * P, COLS)], (UK, COLS)
            phases.append((dict(source=up, size=UNIT), nt // 2, UK))
            phases.append((dict(source=self.unit_sources(w2[t0 * P:(t0 + nt) * P], nt // 4), size=nt // 4 * COLS), 4, nt // 4))
        for n, (phase, pairs, kt) in enumerate(phases):
            after = phases[n + 1][0] if n + 1 < len(phases) else following
            if n % 2 == 0:
                prepare = None if n else Normed(self, 6 * layer + 3, 6 * layer + 4)
                self.linear("up", phase, pairs, after, (self.act_hi, self.act_lo), prepare, Glu(self, pairs), pieces[n])
            else:
                self.linear("down", phase, pairs, after, (self.hid_hi, self.hid_lo), None, AddGated(self, 6 * layer + 5, n == 5),
                            pieces[n], kt)

    def ffn_first(self, layer):
        w1, w3 = (self.i[n][layer].rearrange("(k p) n -> p k n", p=P) for n in ("f_w1", "f_w3"))

        def up(i, u):
            q = u % 4
            return (w1 if u < 4 else w3)[:, q * UK:(q + 1) * UK, bass.ds(i * COLS, COLS)], (UK, COLS)
        return dict(source=up, size=UNIT)

    def index_key(self, following):
        nc, s, ps = self.nc, self.s, self.ps
        s0, p0 = self.split_units, self.pairs
        self.split_units += 8
        self.pairs += 1
        n = 2 * 136
        with nc.Block() as block:
            @block.sync
            def _(sp):
                for u in range(RAW):
                    sp.wait_ge(s("unit_split"), s0 + u + 1)
                    self.load_unit(sp, u, following["source"](0, u))

            @block.scalar
            def _(act):
                for u in range(RAW):
                    self.split_hi(act, 0, u, s0, p0, n)
                act.wait_ge(s("unit_used"), s0 + 8)
                nc.scalar.activation(self.kiw[:], ps[:, 4:6, 0:T], ACT.Copy).then_inc(s("kiw"), 1)

            @block.vector
            def _(dve):
                for u in range(RAW):
                    self.split_lo(dve, 0, u, s0, n)

            @block.tensor
            def _(pe):
                for u in range(RAW):
                    pe.wait_ge(s("unit_split"), s0 + u + 1)
                    self.multiply(u, 2, 2 * u, KT, 136, ((0, P), (8, 136)), self.act_hi, self.act_lo, (4, 5)).then_inc(s("unit_used"), 1)

    def index(self):
        nc, s, ps = self.nc, self.s, self.ps
        width = (P, T)
        jobs = [(qt, h) for h in range(IH) for qt in range(2)]
        barr = (self.barr[:, 0:P], self.barr[:, P:P + T])

        with nc.Block() as block:
            @block.scalar
            def _(act):
                for c in range(5):
                    if c >= 2:
                        act.wait_ge(s("isq_used"), c - 1)
                    src = self.proj[:, 16 + c, :] if c < 4 else self.kiw[:, 0, :]
                    nc.scalar.activation(self.tmp[:, c % 2, :], src, ACT.Square).then_inc(s("isq"), 1)
                for n, (bank, scale, dst) in enumerate(((6, 1.0 / KVR, self.rstd[:]), (7, 1.0 / P, self.tmp[:, 0, :]))):
                    act.wait_ge(s("isq_used"), 5)
                    nc.scalar.activation(dst, ps[:, bank, 0:T], ACT.Ln, scale=scale, bias=self.cst[:, 0:1]).then_inc(s("iln"), 1)
                    act.wait_ge(s("iln"), n + 1)
                    nc.scalar.activation(dst, dst, ACT.Exp, scale=-0.5).then_inc(s("irstd"), 1)
                for kt in range(2):
                    act.wait_ge(s("ckv_turned"), kt + 1)
                    nc.scalar.activation(self.ckvt[:, kt, :], ps[:, kt, :], ACT.Copy).then_inc(s("ckvt"), 1)
                for n, (qt, h) in enumerate(jobs):
                    act.wait_ge(s("rel"), n + 1)
                    if n >= 2:
                        act.wait_ge(s("scored"), n - 1)
                    nc.scalar.activation(self.rel[:, qt, 0:width[qt]], ps[:, 2 + n % 4, 0:width[qt]], ACT.Relu).then_inc(s("relu"), 1)

            @block.vector
            def _(dve):
                self.arm(dve, HEADS_ARMED)
                dve.wait_ge(s("irstd"), 1)
                for c in range(4):
                    nc.vector.scalar_tensor_tensor(self.ckvn[:, c, :], self.proj[:, 16 + c, :], self.pv[:, PV_KVN + c:PV_KVN + c + 1],
                                                   self.rstd[:], MUL, MUL).then_inc(s("ckvn"), 1)
                dve.wait_ge(s("irstd"), 2)
                nc.vector.scalar_tensor_tensor(self.kiw[:, 0, :], self.kiw[:, 0, :], self.pv[:, PV_KIN:PV_KIN + 1],
                                               self.tmp[:, 0, :], MUL, MUL).then_inc(s("kidx"), 1)
                dve.wait_ge(s("wq_turned"), 1)
                for qt in range(2):
                    nc.vector.tensor_scalar(self.wq[:, qt, :], ps[:, 7, qt * P + 120:qt * P + P], IDX_SCALE, None, MUL).then_inc(s("wq"), 1)
                dve.wait_ge(s("wq"), 2)
                for n, (qt, h) in enumerate(jobs):
                    dve.wait_ge(s("relu"), n + 1)
                    o, r, wcol = self.sco[:, qt, 0:width[qt]], self.rel[:, qt, 0:width[qt]], self.wq[:, qt, h:h + 1]
                    if h == 0:
                        nc.vector.tensor_scalar(o, r, wcol, None, MUL).then_inc(s("scored"), 1)
                    else:
                        dve.wait_ge(s("scored"), n - 1)
                        nc.vector.scalar_tensor_tensor(o, r, wcol, o, MUL, ADD).then_inc(s("scored"), 1)
                dve.wait_ge(s("scored"), len(jobs))
                for qt in range(2):
                    nc.vector.memset(self.sco[0:HD, qt, width[qt] - C:width[qt]], NEG).then_inc(s("limited"), 1)
                dve.wait_ge(s("limited"), 2)
                for n in range(TOPK // 8):
                    for qt in range(2):
                        src = (self.wrk if n else self.sco)[:, qt, 0:width[qt]]
                        if n:
                            dve.wait_ge(s("taken"), 2 * (n - 1) + qt + 1)
                        nc.vector.max(self.top8[:, qt, :], src).then_inc(s("top8"), 1)
                    for qt in range(2):
                        src = (self.wrk if n else self.sco)[:, qt, 0:width[qt]]
                        dve.wait_ge(s("top8"), 2 * n + qt + 1)
                        nc.vector.match_replace(self.wrk[:, qt, 0:width[qt]], self.top8[:, qt, :], src, TAKEN).then_inc(s("taken"), 1)
                for qt in range(2):
                    dve.wait_ge(s("taken"), TOPK // 4 - 1 + qt)
                    nc.vector.tensor_scalar(barr[qt], self.wrk[:, qt, 0:width[qt]], TAKEN, BAR, ALU.not_equal, MUL).then_inc(s("barred"), 1)

            @block.tensor
            def _(pe):
                for c in range(5):
                    pe.wait_ge(s("isq"), c + 1)
                    nc.tensor.matmul(ps[:, 6 + c // 4, 0:T], self.ones[:], self.tmp[:, c % 2, :], start=c % 4 == 0,
                                     stop=c >= 3).then_inc(s("isq_used"), 1)
                pe.wait_ge(s("iln"), 2)
                for qt in range(2):
                    last = nc.tensor.transpose(ps[:, 7, qt * P:(qt + 1) * P], self.kiw[:, 1, qt * P:(qt + 1) * P], self.ident[:])
                last.then_inc(s("wq_turned"), 1)
                for kt in range(2):
                    for c in range(4):
                        pe.wait_ge(s("ckvn"), c + 1)
                        last = nc.tensor.transpose(ps[:, kt, c * P:(c + 1) * P], self.ckvn[:, c, kt * P:(kt + 1) * P], self.ident[:])
                    last.then_inc(s("ckv_turned"), 1)
                pe.wait_ge(s("kidx"), 1)
                for n, (qt, h) in enumerate(jobs):
                    if n >= 4:
                        pe.wait_ge(s("relu"), n - 3)
                    nc.tensor.matmul(ps[:, 2 + n % 4, 0:width[qt]], self.proj[:, 20 + h, qt * P:(qt + 1) * P],
                                     self.kiw[:, 0, 0:width[qt]], start=True, stop=True).then_inc(s("rel"), 1)

    def heads(self):
        nc, s, ps, A = self.nc, self.s, self.ps, self.A
        parts = (slice(0, P), slice(P, P + T))

        with nc.Block() as block:
            @block.sync
            def _(sp):
                with sp.Fori(0, HEADS // 2) as i:
                    for j in range(2):
                        sp.wait_ge(s("uk_turned"), i * 2 + 1)
                        sp.dma_start(A[j]["uk"][:], self.i["b_w_uk"][0][bass.ds(i * 2 + j, 1)].rearrange("h d c -> d (h c)")).then_inc(s(f"uk_loaded{j}"), 16)
                        sp.wait_ge(s("vhp"), i * 2 + 1)
                        sp.dma_start(A[j]["uv"][:], self.i["b_w_uv"][0][bass.ds(i * 2 + j, 1)].rearrange("h (c p) d -> p (h c) d", p=P)).then_inc(s(f"uv_loaded{j}"), 16)

            @block.scalar
            def _(act):
                with act.Fori(0, HEADS // 2) as i:
                    def w(name, j):
                        act.wait_ge(s(name), i * 2 + (j + 1 + one(name)))
                    for j in range(2):
                        act.wait_ge(s("logits"), i * 2 + 1)
                        nc.scalar.activation(A[j]["qc"][:].unsqueeze(1), self.proj[:, bass.ds(i * 2 + j, 1), :], ACT.Copy).then_inc(s("qc"), 1)
                    for j in range(2):
                        w("uk_turned", j)
                        nc.scalar.activation(A[j]["ukT"][:].rearrange("p c d -> p (c d)"), ps[:, 4 * j, :], ACT.Copy).then_inc(s("ukT"), 1)
                    for j in range(2):
                        w("vhp", j)
                        nc.scalar.activation(A[j]["vh"][:].rearrange("p k d -> p (k d)"), ps[:, 4 * j + 2, 0:T], ACT.Copy).then_inc(s("vh"), 1)
                    for j in range(2):
                        b = A[j]
                        w("negmax", j)
                        act.wait_ge(s("probs"), i * 2 + 1)
                        for qt in range(2):
                            last = nc.scalar.activation(b["lgf"][:, parts[qt]], b["lgf"][:, parts[qt]], ACT.Exp, bias=b["st"][:, 2 + qt:3 + qt],
                                                        scale=ATT_SCALE, accum_out=b["st"][:, 4 + qt:5 + qt])
                        last.then_inc(s("exps"), 1)
                    for j in range(2):
                        w("pturned", j)
                        nc.scalar.activation(A[j]["pT"][:].rearrange("p k q -> p (k q)"), ps[:, 4 * j, 0:3 * P], ACT.Copy).then_inc(s("pT"), 1)
                    for j in range(2):
                        w("outp", j)
                        nc.scalar.activation(self.hid_hi[:, bass.ds(i * 2 + j, 1), :], ps[:, 4 * j + 1:4 * j + 2, 0:T], ACT.Copy).then_inc(s("o_hi"), 1)

            @block.vector
            def _(dve):
                with dve.Fori(0, HEADS // 2) as i:
                    def w(name, j):
                        dve.wait_ge(s(name), i * 2 + (j + 1 + one(name)))
                    for j in range(2):
                        w("khp", j)
                        nc.vector.tensor_copy(A[j]["kh"][:], ps[:, 4 * j + 1, 0:T]).then_inc(s("kh"), 1)
                    for j in range(2):
                        b = A[j]
                        w("logits", j)
                        dve.wait_ge(s("probs"), i * 2 + 1)
                        nc.vector.tensor_tensor(b["lgf"][:], ps[:, 4 * j + 3, 0:3 * P], self.barr[:], ADD).then_inc(s("barred_logits"), 1)
                        w("barred_logits", j)
                        for qt in range(2):
                            last = nc.vector.reduce_max(b["st"][:, qt:qt + 1], b["lgf"][:, parts[qt]], AX)
                        last.then_inc(s("maxes"), 1)
                        w("maxes", j)
                        nc.vector.tensor_scalar(b["st"][:, 2:4], b["st"][:, 0:2], -ATT_SCALE, None, MUL).then_inc(s("negmax"), 1)
                    for j in range(2):
                        b = A[j]
                        w("exps", j)
                        nc.vector.reciprocal(b["st"][:, 6:8], b["st"][:, 4:6]).then_inc(s("recip"), 1)
                        w("recip", j)
                        dve.wait_ge(s("pturned"), i * 2 + 1)
                        for qt in range(2):
                            last = nc.vector.tensor_scalar(b["prf"][:, parts[qt]], b["lgf"][:, parts[qt]], b["st"][:, 6 + qt:7 + qt], None, MUL)
                        last.then_inc(s("probs"), 1)
                    for j in range(2):
                        w("o_hi", j)
                        m = bass.ds(i * 2 + j, 1)
                        nc.vector.tensor_tensor(self.hid_lo[:, m, :], ps[:, 4 * j + 1:4 * j + 2, 0:T], self.hid_hi[:, m, :].bitcast(F32),
                                                SUB).then_inc(s("o_lo"), 1)

            @block.tensor
            def _(pe):
                with pe.Fori(0, HEADS // 2) as i:
                    def w(name, j):
                        pe.wait_ge(s(name), i * 2 + (j + 1 + one(name)))
                    for j in range(2):
                        pe.wait_ge(s(f"uk_loaded{j}"), i * 16 + 16)
                        pe.wait_ge(s("pT"), i * 2 + 1)
                        for c in range(4):
                            last = nc.tensor.transpose(ps[:, 4 * j, c * P:(c + 1) * P], A[j]["uk"][:, c * P:(c + 1) * P], self.ident[:])
                        last.then_inc(s("uk_turned"), 1)
                    for j in range(2):
                        pe.wait_ge(s(f"uv_loaded{j}"), i * 16 + 16)
                        pe.wait_ge(s("vh"), i * 2 + 1)
                        for kt in range(2):
                            for c in range(4):
                                last = nc.tensor.matmul(ps[:, 4 * j + 2, kt * P:(kt + 1) * P], self.ckvn[:, c, kt * P:(kt + 1) * P],
                                                        A[j]["uv"][:, c, :], start=c == 0, stop=c == 3)
                        last.then_inc(s("vhp"), 1)
                    for j in range(2):
                        w("ukT", j)
                        pe.wait_ge(s("o_lo"), i * 2 + 1)
                        for c in range(4):
                            last = nc.tensor.matmul(ps[:, 4 * j + 1, 0:T], A[j]["ukT"][:, c, :], self.ckvn[:, c, :], start=c == 0, stop=c == 3)
                        last.then_inc(s("khp"), 1)
                    for j in range(2):
                        b = A[j]
                        w("kh", j)
                        w("qc", j)
                        pe.wait_ge(s("barred_logits"), i * 2 + 1)
                        nc.tensor.matmul(ps[:, 4 * j + 3, 0:P], b["qc"][:, 0:P], b["kh"][:, 0:P], start=True, stop=True)
                        nc.tensor.matmul(ps[:, 4 * j + 3, P:P + T], b["qc"][:, P:T], b["kh"][:], start=True, stop=True).then_inc(s("logits"), 1)
                    for j in range(2):
                        w("probs", j)
                        for n, col in enumerate((0, P, 2 * P)):
                            last = nc.tensor.transpose(ps[:, 4 * j, n * P:(n + 1) * P], A[j]["prf"][:, col:col + P], self.ident[:])
                        last.then_inc(s("pturned"), 1)
                    for j in range(2):
                        b = A[j]
                        w("pT", j)
                        w("vh", j)
                        pT = b["pT"][:].rearrange("p k q -> p (k q)")
                        nc.tensor.matmul(ps[:, 4 * j + 1, 0:T], b["vh"][:, 0, :], pT[:, 0:T], start=True, stop=False)
                        nc.tensor.matmul(ps[:, 4 * j + 1, P:T], b["vh"][:, 1, :], pT[:, T:T + P], start=False, stop=True).then_inc(s("outp"), 1)

    def final(self):
        nc, s, ps = self.nc, self.s, self.ps
        n0 = self.norms
        with nc.Block(no_gpsimd_drain=True) as block:
            @block.scalar
            def _(act):
                self.rstd_from_sums(act, n0)
                for k in range(0, KT, 2):
                    act.wait_ge(s("out_turned"), k + 1)
                    nc.scalar.activation(self.fin[:, :, k * P:(k + 1) * P], ps[:, k % 4, 0:T].rearrange("p (a n) -> p a n", a=2),
                                         ACT.Copy).then_inc(s("out_even"), 1)

            @block.vector
            def _(dve):
                dve.wait_ge(s("rstd"), n0 + 1)

                def take(k):
                    dve.wait_ge(s("out_turned"), k + 1)
                    nc.vector.tensor_copy(self.fin[:, :, k * P:(k + 1) * P],
                                          ps[:, k % 4, 0:T].rearrange("p (a n) -> p a n", a=2)).then_inc(s("out_odd"), 1)
                for k in range(KT):
                    if k >= 2:
                        dve.wait_ge(s("out_turned"), k - 1)
                    nc.vector.scalar_tensor_tensor(self.nt[:, k % 2, :], self.x[:, k, :], self.pv[:, PV_FN + k:PV_FN + k + 1],
                                                   self.rstd[:], MUL, MUL).then_inc(s("out_normed"), 1)
                    if k % 2 == 0 and k:
                        take(k - 1)
                take(KT - 1)

            @block.tensor
            def _(pe):
                self.sum_squares(pe, n0)
                for k in range(KT):
                    pe.wait_ge(s("out_normed"), k + 1)
                    if k >= 4:
                        pe.wait_ge(s("out_even") if k % 2 == 0 else s("out_odd"), (k - 4) // 2 + 1)
                    for a in range(2):
                        last = nc.tensor.transpose(ps[:, k % 4, a * P:(a + 1) * P], self.nt[:, k % 2, a * P:(a + 1) * P], self.ident[:])
                    last.then_inc(s("out_turned"), 1)

            @block.sync
            def _(sp):
                for q in range(4):
                    sp.wait_ge(s("out_even"), 2 * q + 2)
                    sp.wait_ge(s("out_odd"), 2 * q + 2)
                    at = slice(q * 512, (q + 1) * 512)
                    sp.dma_start(self.out[0].rearrange("(a p) d -> p a d", p=P)[:, :, at], self.fin[:, :, at]).then_inc(s("out_stored"), 16)
                sp.wait_ge(s("out_stored"), 64)

    def build(self):
        I = self.i
        rkv = [dict(source=self.unit_sources(I["a_w_rkv"][0, q]), size=UNIT) for q in range(3)]
        w1, a1, g1 = (I[n][0].rearrange("(k p) n -> p k n", p=P) for n in ("a_w1", "a_a1", "a_g1"))

        def lora_inner(i, u):
            if u < 2 or u >= 6:
                return (w1 if u < 2 else a1)[:, (u % 2) * 8:(u % 2 + 1) * 8, :], (8, 96)
            return g1[:, (u - 2) * 4:(u - 1) * 4, :], (4, 256)
        w_o = dict(source=self.unit_sources(I["a_w_o"][0]))
        self.prologue(rkv[0])
        if self.stop == 0:
            return
        local = [n for n in self.sems if n in PROLOGUE_ONLY or n.startswith("first_loaded")]
        self.nc.clear_and_free_semaphores([self.sems.pop(n) for n in local])
        self.modulate_first()
        halves = ((self.act_hi, self.act_lo), (self.hid_hi, self.hid_lo), (self.act_hi, self.act_lo))
        mixed = Mixed(self, 0, *halves[0])
        for q in range(3):
            after = Mixed(self, (2, 3)[q], *halves[q + 1]) if q < 2 else MixedWhole(self, [(1, self.lmix[0]), (5, self.lmix[2])])
            self.linear("rkv"[q], rkv[q], 4, rkv[q + 1] if q < 2 else dict(source=lora_inner), halves[q], mixed if q == 0 else None,
                        ToScratch(self, q, 4), beside=(after,))
        self.loras(w_o)
        if self.stop == 1:
            return
        self.s("sums_zeroed")
        kept = set(self.sems) - set(RWKV_ARMED) | {"ada_loaded0", "ada_loaded1", "sums_zeroed"}
        self.rwkv()
        local = [n for n in self.sems if n not in kept]
        self.nc.clear_and_free_semaphores([self.sems.pop(n) for n in local])
        if self.stop == 2:
            return
        hid = (self.hid_hi, self.hid_lo)
        self.linear("w_o", w_o, 4, self.ffn_first(0), hid, None, AddGated(self, 2, True), first_loaded=EARLY)
        if self.stop == 3:
            return
        w_in = I["b_w_in"][0]
        dsa_in = dict(source=self.unit_sources(w_in[:, 0:3584]), size=UNIT)
        tail_view = w_in.rearrange("(k p) n -> p k n", p=P)
        dsa_tail = dict(source=lambda i, u: (tail_view[:, 2 * u:2 * u + 2, 3584:3720], (2, 136)))
        b_w_o = dict(source=self.unit_sources(I["b_w_o"][0]))
        self.ffn(0, [[(0, 8, 96, 2)], [(0, 4, 112, 2)], [(0, 4, 120, 2), (4, 8, 128, 2)], [(0, 4, 136, 2)],
                     [(0, 6, 144, 2)], [(0, 2, 156, 2), (2, 4, 160, 2)]], dsa_in)
        if self.stop == 4:
            return
        self.linear("dsa", dsa_in, 7, dsa_tail, (self.act_hi, self.act_lo), Normed(self, 6, 7), ToProj(self), [(0, 6, 164, 2)])
        self.index_key(b_w_o)
        if self.stop == 5:
            return
        self.index()
        self.heads()
        self.linear("b_w_o", b_w_o, 4, self.ffn_first(1), hid, None, AddGated(self, 8, True))
        if self.stop == 6:
            return
        self.ffn(1, [[(0, 8, 176, 2)]] + [()] * 5, None)
        if self.stop == 7:
            return
        self.final()


INPUTS = ["x", "c", "ada_w", "ada_b", "a_mu", "a_w_rkv", "a_w0", "a_w1", "a_w2", "a_a0", "a_a1", "a_a2", "a_g1", "a_g2",
          "a_k_k", "a_k_a", "a_r_k", "a_ln_w", "a_ln_b", "a_w_o", "b_w_in", "b_kv_norm", "b_kidx_norm", "b_w_uk",
          "b_w_uv", "b_w_o", "f_w1", "f_w3", "f_w2", "final_norm"]


def build(nc, ins, out, stop=99):
    with ExitStack() as ctx:
        p = Program(nc, ctx, ins, out)
        p.stop = stop
        p.build()
        return p


def kernel(**inputs):
    import numpy as np
    from concourse import bacc
    from concourse.bass_utils import run_bass_kernel_spmd

    nc = bacc.Bacc("TRN2", target_bir_lowering=False, num_devices=1)
    arrays, aps = {}, {}
    for name in INPUTS:
        a = np.ascontiguousarray(inputs[name])
        arrays["in_" + name] = a
        aps[name] = nc.dram_tensor("in_" + name, a.shape, mybir.dt.from_np(a.dtype), kind="ExternalInput").ap()
    out = nc.dram_tensor("out", (1, T, D), F32, kind="ExternalOutput").ap()
    build(nc, aps, out)
    r = run_bass_kernel_spmd(nc, [arrays], core_ids=[0])
    return r.results[0]["out"]
```
